# Optimizing a Trainium2 kernel written in Bass

```python
import math
import jax, jax.numpy as jnp
from jax import lax
import numpy as np

D_MODEL = 1024
BATCH = 1
SEQ = 1024
DEPTH = 2

GRID_W = 64
D_MIX = D_MODEL
DA_HEAD_DIM = 64
DA_WIDTH = D_MIX // 2
DA_HEADS = DA_WIDTH // (2 * DA_HEAD_DIM)
NA_HEAD_DIM = 64
NA_WIDTH = D_MIX - DA_WIDTH
NA_HEADS = NA_WIDTH // NA_HEAD_DIM
NA_ROWS_MAX = 8
NA_COLS = 16
NA_COL_BLOCK = 16
NA_KEY_COLS = NA_COL_BLOCK + NA_COLS
Q_BLOCK = 128
RMS_EPS = 1e-6
SPLITS = (DA_WIDTH, DA_WIDTH, DA_WIDTH, NA_WIDTH, NA_WIDTH, NA_WIDTH, D_MIX)
IN_WIDTH = sum(SPLITS)

kernel_name = "hybrid_diffattn_natten2d_encoder"

def rms_norm(x, g):
    xf = x.astype(jnp.float32)
    y = xf * lax.rsqrt(jnp.mean(xf * xf, axis=-1, keepdims=True) + RMS_EPS)
    return (y * g.astype(jnp.float32)).astype(x.dtype)

def alibi_slopes(n_heads):
    return jnp.asarray(2.0 ** (-8.0 * np.arange(1, n_heads + 1) / n_heads), dtype=jnp.float32)

def diff_attention(q, k, v, lam, lam_init, subln_g):
    B, S, H, _, dh = q.shape
    nb = S // Q_BLOCK
    qb = q.reshape(B, nb, Q_BLOCK, H, 2, dh).transpose(1, 0, 2, 3, 4, 5)
    slopes = alibi_slopes(H)
    kpos = jnp.arange(S)
    scale = dh ** -0.5

    def block(args):
        qi, i = args
        s = jnp.einsum('bqhcd,bkhcd->bhcqk', qi, k,
                       preferred_element_type=jnp.float32) * scale
        qpos = i * Q_BLOCK + jnp.arange(Q_BLOCK)
        dist = jnp.abs(qpos[:, None] - kpos[None, :]).astype(jnp.float32)
        s = s - slopes[None, :, None, None, None] * dist[None, None, None]
        p = jax.nn.softmax(s, axis=-1)
        a = p[:, :, 0] - lam * p[:, :, 1]
        return jnp.einsum('bhqk,bkhe->bqhe', a.astype(v.dtype), v)

    o = lax.map(block, (qb, jnp.arange(nb)))
    o = o.transpose(1, 0, 2, 3, 4).reshape(B, S, H, 2 * dh)
    o = rms_norm(o, subln_g) * (1.0 - lam_init)
    return o.reshape(B, S, H * 2 * dh)

def neighbourhood_attention(q, k, v, rpb):
    B, S, H, d = q.shape
    rows = S // GRID_W
    kr = min(NA_ROWS_MAX, rows)
    qg = q.reshape(B, rows, GRID_W, H, d)
    kg = k.reshape(B, rows, GRID_W, H, d)
    vg = v.reshape(B, rows, GRID_W, H, d)
    nbk = GRID_W // NA_COL_BLOCK
    qcol = np.arange(GRID_W).reshape(nbk, NA_COL_BLOCK)
    qcstart = np.clip(qcol - NA_COLS // 2, 0, GRID_W - NA_COLS)
    kcstart = np.clip(qcol[:, 0] - NA_COLS // 2, 0, GRID_W - NA_KEY_COLS)
    kcol = kcstart[:, None] + np.arange(NA_KEY_COLS)
    col_valid = ((kcol[:, None, :] >= qcstart[:, :, None]) &
                 (kcol[:, None, :] < qcstart[:, :, None] + NA_COLS))
    dc_idx = np.clip(kcol[:, None, :] - qcol[:, :, None],
                     -(NA_COLS - 1), NA_COLS - 1) + NA_COLS - 1
    col_bias = rpb[:, :, dc_idx]
    scale = d ** -0.5

    def row(r):
        rs = jnp.clip(r - kr // 2, 0, rows - kr)
        krows = lax.dynamic_slice_in_dim(kg, rs, kr, axis=1)
        vrows = lax.dynamic_slice_in_dim(vg, rs, kr, axis=1)
        kb = krows[:, :, kcol]
        vb = vrows[:, :, kcol]
        qr = lax.dynamic_index_in_dim(qg, r, axis=1, keepdims=False)
        qr = qr.reshape(B, nbk, NA_COL_BLOCK, H, d)
        s = jnp.einsum('bnqhd,brnkhd->bhnqrk', qr, kb,
                       preferred_element_type=jnp.float32) * scale
        dr_idx = rs + jnp.arange(kr) - r + NA_ROWS_MAX - 1
        bias = jnp.take(col_bias, dr_idx, axis=1).transpose(0, 2, 3, 1, 4)
        s = s + bias[None].astype(jnp.float32)
        s = jnp.where(col_valid[None, None, :, :, None, :], s, -jnp.inf)
        shp = s.shape
        p = jax.nn.softmax(s.reshape(B, H, nbk, NA_COL_BLOCK, kr * NA_KEY_COLS), axis=-1).reshape(shp)
        o = jnp.einsum('bhnqrk,brnkhd->bnqhd', p.astype(v.dtype), vb)
        return o.reshape(B, GRID_W, H * d)

    out = lax.map(row, jnp.arange(rows))
    return out.transpose(1, 0, 2, 3).reshape(B, S, H * d)

def hybrid_layer(x, g, w_in, w_out, lq1, lk1, lq2, lk2, subln_g, rpb, lam_init):
    B, S, _ = x.shape
    h = rms_norm(x, g)
    z = jnp.einsum('bsd,de->bse', h, w_in)
    cuts = [int(c) for c in np.cumsum(SPLITS)[:-1]]
    qd, kd, vd, qn, kn, vn, gate = jnp.split(z, cuts, axis=-1)
    qd = qd.reshape(B, S, DA_HEADS, 2, DA_HEAD_DIM)
    kd = kd.reshape(B, S, DA_HEADS, 2, DA_HEAD_DIM)
    vd = vd.reshape(B, S, DA_HEADS, 2 * DA_HEAD_DIM)
    f32 = jnp.float32
    lam = (jnp.exp(jnp.sum(lq1.astype(f32) * lk1.astype(f32)))
           - jnp.exp(jnp.sum(lq2.astype(f32) * lk2.astype(f32))) + lam_init)
    o_da = diff_attention(qd, kd, vd, lam, lam_init, subln_g)
    qn = qn.reshape(B, S, NA_HEADS, NA_HEAD_DIM)
    kn = kn.reshape(B, S, NA_HEADS, NA_HEAD_DIM)
    vn = vn.reshape(B, S, NA_HEADS, NA_HEAD_DIM)
    o_na = neighbourhood_attention(qn, kn, vn, rpb)
    o = jnp.concatenate([o_da, o_na], axis=-1) * jax.nn.silu(gate)
    return x + jnp.einsum('bse,ed->bsd', o, w_out)

def setup_inputs(seed: int = 0) -> dict:
    key = jax.random.key(seed)
    ks = jax.random.split(key, 12)
    f32 = jnp.float32
    x = jax.random.normal(ks[0], (BATCH, SEQ, D_MODEL), f32)
    norm_g = 1.0 + 0.02 * jax.random.normal(ks[1], (DEPTH, D_MODEL), f32)
    w_in = jax.random.normal(ks[2], (DEPTH, D_MODEL, IN_WIDTH), f32) * D_MODEL ** -0.5
    w_out = jax.random.normal(ks[3], (DEPTH, D_MIX, D_MODEL), f32) * D_MIX ** -0.5
    lam_q1 = 0.1 * jax.random.normal(ks[4], (DEPTH, DA_HEAD_DIM), f32)
    lam_k1 = 0.1 * jax.random.normal(ks[5], (DEPTH, DA_HEAD_DIM), f32)
    lam_q2 = 0.1 * jax.random.normal(ks[6], (DEPTH, DA_HEAD_DIM), f32)
    lam_k2 = 0.1 * jax.random.normal(ks[7], (DEPTH, DA_HEAD_DIM), f32)
    subln_g = 1.0 + 0.02 * jax.random.normal(ks[8], (DEPTH, 2 * DA_HEAD_DIM), f32)
    rpb = 0.02 * jax.random.normal(ks[9], (DEPTH, NA_HEADS, 2 * NA_ROWS_MAX - 1, 2 * NA_COLS - 1), f32)
    final_g = 1.0 + 0.02 * jax.random.normal(ks[10], (D_MODEL,), f32)
    return {"x": x, "norm_g": norm_g, "w_in": w_in, "w_out": w_out,
            "lam_q1": lam_q1, "lam_k1": lam_k1, "lam_q2": lam_q2, "lam_k2": lam_k2,
            "subln_g": subln_g, "rpb": rpb, "final_g": final_g}

def reference(x, norm_g, w_in, w_out, lam_q1, lam_k1, lam_q2, lam_k2, subln_g, rpb, final_g):
    for l in range(DEPTH):
        lam_init = 0.8 - 0.6 * math.exp(-0.3 * l)
        x = hybrid_layer(x, norm_g[l], w_in[l], w_out[l], lam_q1[l], lam_k1[l],
                         lam_q2[l], lam_k2[l], subln_g[l], rpb[l], lam_init)
    return rms_norm(x, final_g)


_drawn_inputs = setup_inputs


def setup_inputs(seed=0):
    import zlib

    import numpy as np

    out = dict(_drawn_inputs(seed))
    spreads = {}
    factors = {'norm_g': 2.976, 'lam_q1': 2.845, 'subln_g': 6.746, 'rpb': 8.0, 'final_g': 2.922}
    for name, (base, spread) in spreads.items():
        noise = np.random.default_rng([zlib.crc32(name.encode()), seed]).standard_normal(out[name].shape)
        drawn = base * np.exp(spread * noise) if base else spread * noise
        out[name] = __import__('jax').numpy.asarray(drawn.astype(out[name].dtype))
    for name, factor in factors.items():
        out[name] = (out[name] * factor).astype(out[name].dtype)
    return out
```

```python
import numpy as np
import concourse.bass as bass
from concourse import mybir
from contextlib import ExitStack

ALU = mybir.AluOpType
ACT = mybir.ActivationFunctionType
F32 = mybir.dt.float32
F32R = mybir.dt.float32r
FP16 = mybir.dt.float16
I32 = mybir.dt.int32

P = 128
HALF = 512
MASKED = -1e30


def hybrid_encoder(nc, x_t, chunks, norm_gain, final_gain, subln_gain, lam_vecs, bias_rows, out_t):
    D, S = x_t.shape
    NT = D // P
    DEPTH = norm_gain.shape[1] // NT
    HD = lam_vecs.shape[3]
    DA_G, NA_G = 4, 4
    GROUPS = DA_G + NA_G
    RB = 2 * 16 - 1
    RR = 15
    W = 64
    CPL = 4 * GROUPS + NT
    EPS = 1e-6
    EDGE = 14
    LAM_INIT = [0.8 - 0.6 * float(np.exp(-0.3 * l)) for l in range(DEPTH)]
    SLOPES = [2.0 ** (-8.0 * (i + 1) / DA_G) for i in range(DA_G)]
    OFF = S - P
    MADE = 9
    CONSTS = 2 + 2 * DEPTH
    V_, K_, G_, Q_ = range(4)

    KEY0 = [0, 0, 0, 2, 4, 6, 8, 8]
    INNER = [2 <= t <= 5 for t in range(NT)]
    WIDTH = [576 if INNER[t] else 512 for t in range(NT)]

    def uses(na):
        order, split = {}, {}
        def use(key, halves):
            order[key] = len(order)
            if halves:
                split[key] = len(split)
        for t in range(NT + 2):
            if t == 0:
                use(("V", 0), True)
                use(("V", 1), True)
            if 1 <= t <= NT:
                for c in range(3 if na and INNER[t - 1] else 2):
                    use(("T", t - 1, c), True)
            if t >= 2:
                use(("U", t - 2), False)
        return order, split
    ORDER = {na: uses(na)[0] for na in (False, True)}
    SPLIT = {na: uses(na)[1] for na in (False, True)}
    ORDERS = DA_G * len(ORDER[False]) + NA_G * len(ORDER[True])
    SPLITS = DA_G * len(SPLIT[False]) + NA_G * len(SPLIT[True])

    class Group:

        def __init__(self, l, na, i, project=True):
            self.l, self.na, self.i, self.project = l, na, i, project
            self.g = i + (DA_G if na else 0)

        def step(self, t):
            return self.l * (GROUPS * NT) + self.g * NT + t

        def kind_step(self, t):
            return self.l * (DA_G * NT) + self.i * NT + t

        def group(self):
            return self.l * GROUPS + self.g

        def use(self, *key):
            first = DA_G * len(ORDER[False]) if self.na else 0
            return self.l * ORDERS + first + self.i * len(ORDER[self.na]) + ORDER[self.na][key]

        def split(self, *key):
            first = DA_G * len(SPLIT[False]) if self.na else 0
            return self.l * SPLITS + first + self.i * len(SPLIT[self.na]) + SPLIT[self.na][key]

        def piece(self, t):
            return self.l * (2 * CPL) + (self.g + 1) * NT + t

        def chunk(self, t):
            return self.l * CPL + (self.g + 1) * 4 + t // 2

    class First(Group):

        def __init__(self, l):
            self.l, self.na, self.i, self.g, self.project = l, False, -1, -1, True

    with ExitStack() as ctx:
        def sb(name, shape, dt=F32):
            return ctx.enter_context(nc.sbuf_tensor(name, shape, dt))

        def sem(name):
            return ctx.enter_context(nc.semaphore(name))

        xt = sb("xt", [P, NT, S])
        h_hi = sb("h_hi", [P, NT, S], F32R)
        h_lo = sb("h_lo", [P, NT, S], F32R)
        w_raw = sb("w_raw", [P, NT, P])
        w_hi = sb("w_hi", [P, 2, NT, P], F32R)
        w_lo = sb("w_lo", [P, 2, NT, P], F32R)
        q_hi = sb("q_hi", [P, S], F32R)
        q_lo = sb("q_lo", [P, S], F32R)
        k_hi = sb("k_hi", [P, S], F32R)
        k_lo = sb("k_lo", [P, S], F32R)
        k_next = sb("k_next", [P, S])
        v_next = sb("v_next", [P, S])
        v_hl = sb("v_hl", [P, NT, 256], F32R)
        gate_next = sb("gate_next", [P, S])
        gate = sb("gate", [P, S])
        gate_exp = sb("gate_exp", [P, HALF])
        prob = sb("prob", [P, 2, 2, S])
        pt_hi = sb("pt_hi", [P, 2, HALF], F32R)
        pt_lo = sb("pt_lo", [P, 2, HALF], F32R)
        px_hi = sb("px_hi", [HD, 256], F32R)
        px_lo = sb("px_lo", [HD, 256], F32R)
        dist = sb("dist", [P, OFF + S], FP16)
        edge = sb("edge", [P, 2, EDGE * W])
        inner = sb("inner", [P, 2, 9 * W])
        mixed = sb("mixed", [P, S])
        u_hi = sb("u_hi", [P, P])
        u = sb("u", [P, 2, P])
        un = sb("un", [P, 2, P])
        ident = sb("ident", [P, P])
        ones = sb("ones", [P, 1])
        colmask = sb("colmask", [P, W])
        ngain = sb("ngain", [P, DEPTH * NT])
        fgain = sb("fgain", [P, NT])
        sgain = sb("sgain", [P, DEPTH])
        qscale = sb("qscale", [P, GROUPS])
        escale = sb("escale", [P, DA_G])
        escale_now = sb("escale_now", [P, 1])
        nescale = sb("nescale", [P, DA_G])
        neglam = sb("neglam", [P, DEPTH])
        mx = sb("mx", [P, 2, 2])
        nm = sb("nm", [P, 2, 2])
        rsum = sb("rsum", [P, 2, 2])
        rrec = sb("rrec", [P, 2, 2])
        cmix = sb("cmix", [P, 2])
        ssq = sb("ssq", [P, 2])
        msq = sb("msq", [P, 2])
        rms = sb("rms", [P, 2])
        power = sb("power", [P, NT])
        stat = sb("stat", [P, NT])
        rinv = sb("rinv", [P, NT])
        lam_s = sb("lam_s", [P, 2, DEPTH])
        lam_e = sb("lam_e", [P, 2, DEPTH])
        squares = prob[:, 0, 0, :]
        square = prob[:, 0, 1, :]
        lam_in = gate[:, 0:4 * DEPTH * HD].rearrange("p (a l d) -> p a l d", a=4, l=DEPTH)
        normed = [prob[:, 1, 0, :], prob[:, 1, 1, :]]

        scores = ctx.enter_context(nc.psum_tensor("scores", [P, 2, S], F32))
        proj = ctx.enter_context(nc.psum_tensor("proj", [P, 2, HALF], F32))
        turn = ctx.enter_context(nc.psum_tensor("turn", [P, HALF], F32))
        mix = ctx.enter_context(nc.psum_tensor("mix", [P, HALF], F32))

        mixed_dram = nc.dram_tensor("mixed_dram", (D, S), F32).ap()
        bias_dram = nc.dram_tensor("bias_dram", (DEPTH * 2 * NA_G, 2, W, EDGE * W), F32).ap()

        x_in = [sem(f"x_in{i}") for i in range(NT)]
        const_in = sem("const_in")
        lam_loaded = sem("lam_loaded")
        bias_spread = sem("bias_spread")
        w_in = sem("w_in")
        edge_in = sem("edge_in")
        mixed_out = sem("mixed_out")
        mixed_in = [sem(f"mixed_in{i}") for i in range(NT)]
        stored = [sem(f"stored{b}") for b in range(2)]
        made = sem("made")
        lam_dot = sem("lam_dot")
        lam_exp = sem("lam_exp")
        consts_done = sem("consts_done")
        dist_int = sem("dist_int")
        w_hi_done = sem("w_hi_done")
        w_lo_done = sem("w_lo_done")
        sq_done = sem("sq_done")
        sum_done = sem("sum_done")
        stat_mm = sem("stat_mm")
        stat_done = sem("stat_done")
        rinv_done = sem("rinv_done")
        spread_mm = sem("spread_mm")
        norm_done = sem("norm_done")
        h_hi_done = sem("h_hi_done")
        h_ready = sem("h_ready")
        piece_done = sem("piece_done")
        piece_half = sem("piece_half")
        piece_freed = sem("piece_freed")
        gate_step = sem("gate_step")
        q_ready = sem("q_ready")
        k_hi_done = sem("k_hi_done")
        k_ready = sem("k_ready")
        gate_ready = sem("gate_ready")
        edge_masked = sem("edge_masked")
        inner_copied = sem("inner_copied")
        inner_ready = sem("inner_ready")
        qk_done = sem("qk_done")
        scores_read = sem("scores_read")
        shift_ready = sem("shift_ready")
        exp_done = sem("exp_done")
        escale_set = sem("escale_set")
        rrec_done = sem("rrec_done")
        cmix_done = sem("cmix_done")
        comb_done = sem("comb_done")
        turned = sem("turned")
        turn_hi = sem("turn_hi")
        turn_freed = sem("turn_freed")
        pv_done = sem("pv_done")
        u_half = sem("u_half")
        u_done = sem("u_done")
        ssq_done = sem("ssq_done")
        msq_done = sem("msq_done")
        rms_done = sem("rms_done")
        un_done = sem("un_done")

        f32 = lambda t: t.bitcast(F32)

        def groups(e, l, attend):
            with e.Fori(0, DA_G) as i:
                attend(Group(l, False, i))
            with e.Fori(0, NA_G - 1) as i:
                attend(Group(l, True, i))
            attend(Group(l, True, NA_G - 1, project=False))

        begun = {e: sem(f"begun_{e}") for e in ("act", "dve", "pe", "pool")}

        def reached(e, count, n):
            e.wait_ge(count, n + 1)

        def start_at_one(e, *counts):
            for count in counts:
                e.sem_inc(count, 1)

        def begin(e, name):
            e.sem_inc(begun[name], 1)

        block = ctx.enter_context(nc.Block())

        @block.sync
        def _(sp):
            start_at_one(sp, mixed_out)
            for i in range(NT):
                sp.dma_start(xt[:, i, :], x_t[i * P:(i + 1) * P, :]).then_inc(x_in[i], 16)
                if i == 0:
                    sp.dma_start(w_raw[:], chunks[0].rearrange("p (t c) -> p t c", c=P)).then_inc(w_in, 16)
            sp.dma_start(ngain[:], norm_gain).then_inc(const_in, 16)
            sp.dma_start(fgain[:], final_gain).then_inc(const_in, 16)
            sp.dma_start(sgain[:], subln_gain).then_inc(const_in, 16)
            sp.dma_start(lam_in, bass.AP(lam_vecs.tensor, 0, [[0, P], [1, 4 * DEPTH * HD]])
                         .rearrange("p (a l d) -> p a l d", a=4, l=DEPTH)).then_inc(lam_loaded, 16)
            for h in range(DEPTH * 2 * NA_G):
                for odd in range(2):
                    first = W + (h * RR + 1 - odd) * RB + 15
                    sp.dma_start(bias_dram[h, odd].rearrange("q (r k) -> r q k", k=W),
                                 bass.AP(bias_rows.tensor, first, [[RB, EDGE], [-1, W], [1, W]]))\
                        .then_inc(bias_spread, 16)

            def load_chunk(c):
                sp.wait_ge(w_lo_done, c)
                sp.dma_start(w_raw[:], chunks[bass.ds(c, 1)].rearrange("o p (t c) -> (o p) t c", c=P))\
                    .then_inc(w_in, 16)

            def load_edge(l, i):
                for hd in range(2):
                    sp.dma_start(edge[:, hd, :], bias_dram[bass.ds(l * 2 * NA_G + 2 * i + hd, 1)]
                                 .rearrange("o r q k -> (o r q) k")).then_inc(edge_in, 16)

            def attend(g):
                if g.project:
                    for j in range(4):
                        load_chunk(g.chunk(2 * j) + 1)
                    if g.na:
                        reached(sp, scores_read, 2 * g.step(NT))
                        load_edge(g.l, g.i + 1)
                else:
                    reached(sp, piece_done, g.l * 2 * CPL + GROUPS * NT)
                    reached(sp, mixed_out, 16 * g.group())
                    for i in range(NT - 1):
                        sp.dma_start(f32(h_lo[:, i, :]), mixed_dram[i * P:(i + 1) * P, :])\
                            .then_inc(mixed_in[i], 16)
                reached(sp, turn_freed, g.use("U", NT - 1) + 1)
                sp.dma_start(mixed_dram[bass.ds(g.g * P, P), :], mixed[:]).then_inc(mixed_out, 16)

            with sp.Fori(0, DEPTH) as l:
                sp.wait_ge(bias_spread, 16 * DEPTH * 4 * NA_G)
                reached(sp, scores_read, 2 * l * GROUPS * NT)
                load_edge(l, 0)
                for j in range(4):
                    load_chunk(First(l).chunk(2 * j) + 1)
                groups(sp, l, attend)
                last = NT - 1
                reached(sp, mixed_out, 16 * (l + 1) * GROUPS)
                sp.dma_start(f32(h_lo[:, last, :]), mixed_dram[last * P:, :]).then_inc(mixed_in[last], 16)
                for j in range(NT - 1):
                    load_chunk(l * CPL + 4 * GROUPS + j + 1)
                sp.wait_ge(w_lo_done, (l + 1) * CPL)
                sp.dma_start(w_raw[:], chunks[bass.ds((l + 1) * CPL, 1)].rearrange("o p (t c) -> (o p) t c", c=P))\
                    .then_inc(w_in, 16)
            for i in range(NT):
                sp.wait_ge(norm_done, DEPTH * NT + i + 1)
                sp.dma_start(out_t[i * P:(i + 1) * P, :], normed[i % 2]).then_inc(stored[i % 2], 16)
            for b in range(2):
                sp.wait_ge(stored[b], 16 * NT // 2)
            sp.wait_ge(w_in, 16 * (DEPTH * CPL + 1))
            sp.wait_ge(const_in, 48)

        @block.gpsimd
        def _(pool):
            pool.memset(ident[:], 0.0).then_inc(made, 1)
            pool.memset(colmask[:], 0.0).then_inc(made, 1)
            pool.memset(ones[:], 1.0).then_inc(made, 1)
            pool.memset(power[:], -0.5).then_inc(made, 1)
            for i in range(DA_G):
                pool.memset(qscale[:, i:i + 1], HD ** -0.5 / SLOPES[i])
                pool.memset(escale[:, i:i + 1], SLOPES[i])
                pool.memset(nescale[:, i:i + 1], -SLOPES[i])
            pool.memset(qscale[:, DA_G:], HD ** -0.5)
            table = prob[:, 1].bitcast(I32).rearrange("p m s -> p (m s)")[:, 0:OFF + S]
            pool.iota(table, pattern=[[1, OFF + S]], base=-OFF, channel_multiplier=-1).then_inc(dist_int, 1)
            pool.wait_ge(made, 4)
            pool.affine_select(out=ident[:], in_=ident[:], compare_op=ALU.not_equal, fill=1.0, base=0,
                               pattern=[[-1, P]], channel_multiplier=1).then_inc(made, 1)
            n = 5
            for first, base, sign in ((0, 8, 1), (16, 7 - 16, -1)):
                for r in range(2):
                    part = colmask[r * W:(r + 1) * W, first:first + 48]
                    pool.wait_ge(made, n)
                    pool.affine_select(out=part, in_=part, compare_op=ALU.is_ge, fill=MASKED, base=base,
                                       pattern=[[sign, 48]], channel_multiplier=-sign).then_inc(made, 1)
                    n += 1
            pool.wait_ge(made, MADE)

            def w_lo_part(c, b):
                pool.wait_ge(w_hi_done, c + 1)
                pool.tensor_tensor(w_lo[:, b], w_raw[:], f32(w_hi[:, b]), ALU.subtract).then_inc(w_lo_done, 1)

            def mask_edge(l, i):
                pool.wait_ge(edge_in, 32 * (l * NA_G + i + 1))
                pool.wait_ge(made, MADE)
                rows = edge[:].rearrange("p h (r k) -> p (h r) k", k=W)
                pool.tensor_tensor(rows, rows, colmask[:].unsqueeze(1).to_broadcast([P, 2 * EDGE, W]), ALU.add)\
                    .then_inc(edge_masked, 1)

            def k_lo_part(n):
                pool.wait_ge(k_hi_done, n + 1)
                pool.tensor_tensor(k_lo[:], k_next[:], f32(k_hi[:]), ALU.subtract).then_inc(k_ready, 1)

            def normalise(g, t):
                b, n = t % 2, g.kind_step(t)
                pool.wait_ge(ssq_done, n + 1)
                begin(pool, "pool")
                pool.tensor_scalar(msq[:, b:b + 1], ssq[:, b:b + 1], 1.0 / P, EPS, ALU.mult, ALU.add)\
                    .then_inc(msq_done, 1)
                pool.wait_ge(msq_done, n + 1)
                pool.tensor_tensor(rms[:, b:b + 1], msq[:, b:b + 1], power[:, 0:1], ALU.pow).then_inc(rms_done, 1)
                pool.wait_ge(rms_done, n + 1)
                begin(pool, "pool")
                pool.tensor_scalar(un[:, b, :], u[:, b, :], rms[:, b:b + 1], None, ALU.mult).then_inc(un_done, 1)

            def attend(g):
                for t in range(NT + 1):
                    if g.project and t < NT and t % 2 == 0:
                        w_lo_part(g.chunk(t) + 1, (t // 2 + 1) % 2)
                    if not g.na and t >= 1:
                        normalise(g, t - 1)
                    if g.project and t == NT - 1:
                        k_lo_part(g.group() + 1)
                if g.na and g.project:
                    mask_edge(g.l, g.i + 1)

            def norm_stats(n):
                pool.wait_ge(stat_done, n + 1)
                pool.tensor_tensor(rinv[:], stat[:], power[:], ALU.pow).then_inc(rinv_done, 1)

            def add_square(n, cols):
                pool.wait_ge(sq_done, n + 1)
                pool.tensor_tensor(squares[:, cols], squares[:, cols], square[:, cols], ALU.add)\
                    .then_inc(sum_done, 1)

            for i in range(NT):
                for hf in range(2):
                    cols = slice(hf * HALF, (hf + 1) * HALF)
                    if i == 0:
                        pool.wait_ge(sq_done, hf + 1)
                        pool.nop().then_inc(sum_done, 1)
                    else:
                        add_square(2 * i + hf, cols)
            with pool.Fori(0, DEPTH) as l:
                w_lo_part(l * CPL, 0)
                norm_stats(l)
                first = First(l)
                for j in range(4):
                    w_lo_part(first.chunk(2 * j) + 1, (j + 1) % 2)
                k_lo_part(l * GROUPS)
                mask_edge(l, 0)
                groups(pool, l, attend)
                for j in range(NT):
                    if j < NT - 1:
                        w_lo_part(l * CPL + 4 * GROUPS + j + 1, (j + 1) % 2)
                    for hf in range(2):
                        cols = slice(hf * HALF, (hf + 1) * HALF)
                        n = (l + 1) * 2 * NT + 2 * j + hf
                        if j == 0:
                            pool.wait_ge(sq_done, n + 1)
                            pool.nop().then_inc(sum_done, 1)
                        else:
                            add_square(n, cols)
            norm_stats(DEPTH)

        @block.scalar
        def _(act):
            start_at_one(act, exp_done)

            def square_of(n, i, hf):
                cols = slice(hf * HALF, (hf + 1) * HALF)
                dst = squares if i == 0 else square
                if i > 0:
                    act.wait_ge(sum_done, n - 1)
                act.activation(dst[:, cols], xt[:, i, cols], ACT.Square).then_inc(sq_done, 1)

            for i in range(NT):
                act.wait_ge(x_in[i], 16)
                for hf in range(2):
                    square_of(2 * i + hf, i, hf)
            act.wait_ge(lam_dot, 2 * DEPTH)
            act.activation(lam_e[:], lam_s[:], ACT.Exp).then_inc(lam_exp, 1)

            def w_hi_part(c, b, freed):
                act.wait_ge(w_in, 16 * (c + 1))
                reached(act, piece_done, freed)
                act.activation(w_hi[:, b], w_raw[:], ACT.Copy).then_inc(w_hi_done, 1)

            def piece_part(g, t):
                ps, n, kind = proj[:, t % 2], g.piece(t), t // 2
                cols = slice((t % 2) * HALF, (t % 2 + 1) * HALF)
                if kind == G_:
                    reached(act, piece_done, n + 1)
                    act.wait_ge(piece_freed, n)
                    act.activation(gate_exp[:], ps, ACT.Exp, scale=-1.0).then_inc(piece_half, 1)
                if kind == Q_:
                    reached(act, piece_done, n + 1)
                    act.wait_ge(qk_done, g.step(NT))
                    col = qscale[:, bass.ds(g.g + 1, 1)]
                    begin(act, "act")
                    act.activation(q_hi[:, cols], ps, ACT.Copy, scale=col).then_inc(piece_half, 1)

            def k_hi_part(g):
                act.wait_ge(qk_done, g.step(NT))
                act.wait_ge(piece_freed, g.piece(2 * K_ + 1) + 1)
                act.activation(k_hi[:], k_next[:], ACT.Copy).then_inc(k_hi_done, 1)

            def turn_part(g, key, dst, src):
                act.wait_ge(turned, g.use(*key) + 1)
                act.activation(dst, src, ACT.Copy).then_inc(turn_hi, 1)

            def v_part(g, c):
                if g.na:
                    dst = v_hl[:, 4 * c:4 * c + 4].rearrange("p k (h s e) -> p k h s e", h=2, s=2)[:, :, :, 0, :]
                    src = turn[:].rearrange("p (k h e) -> p k h e", k=4, h=2)
                else:
                    dst, src = v_hl[:, 4 * c:4 * c + 4, 0:P], turn[:].rearrange("p (k e) -> p k e", k=4)
                turn_part(g, ("V", c), dst, src)

            def p_part(g, t, c):
                reached(act, pv_done, g.step(t))
                if c == 2:
                    turn_part(g, ("T", t, c), px_hi[:], turn[0:HD, 0:256])
                else:
                    turn_part(g, ("T", t, c), pt_hi[:, c, :], turn[:])

            def exponentials(g, t, m):
                b = t % 2
                act.wait_ge(shift_ready, 2 * g.step(t) + m + 1)
                s = prob[:, b, m, 0:WIDTH[t] if g.na else S]
                scale = 1.0 if g.na else escale_now[:]
                act.activation(s, s, ACT.Exp, bias=nm[:, b, m:m + 1], scale=scale,
                               accum_out=rsum[:, b, m:m + 1]).then_inc(exp_done, 1)

            def output_half(g, t):
                b, n = t % 2, g.step(t)
                reached(act, pv_done, n + 1)
                act.wait_ge(rrec_done, n + 1)
                reached(act, u_done, n)
                if g.na:
                    for m in range(2):
                        last = act.activation(u_hi[:, m * HD:(m + 1) * HD], mix[:, m * P:m * P + HD], ACT.Copy,
                                              scale=rrec[:, b, m:m + 1])
                    last.then_inc(u_half, 1)
                else:
                    act.activation(u_hi[:], mix[:, 0:P], ACT.Copy, scale=rrec[:, b, 0:1]).then_inc(u_half, 1)
                    reached(act, u_done, n + 1)
                    act.activation(u_hi[:], u[:, b, :], ACT.Square, accum_out=ssq[:, b:b + 1]).then_inc(ssq_done, 1)

            def take_mixed(l, i):
                act.wait_ge(mixed_in[i], 16 * (l + 1))
                act.activation(h_hi[:, i, :], f32(h_lo[:, i, :]), ACT.Copy).then_inc(h_hi_done, 1)

            def attend(g):
                if not g.na:
                    n = g.l * DA_G + g.i
                    reached(act, exp_done, 2 * g.step(0))
                    act.activation(escale_now[:], escale[:, bass.ds(g.i, 1)], ACT.Copy).then_inc(escale_set, 1)
                    act.wait_ge(escale_set, n + 1)
                for t in range(NT + 1):
                    if g.project and t < NT and t % 2 == 0:
                        w_hi_part(g.chunk(t) + 1, (t // 2 + 1) % 2, g.piece(t))
                    if t == 0:
                        reached(act, turn_freed, g.use("V", 0))
                        act.wait_ge(piece_freed, g.l * 2 * CPL + g.g * NT + 2 * G_ + 2)
                        act.activation(gate[:], gate_next[:], ACT.Copy).then_inc(gate_ready, 1)
                    for c in range(2):
                        if t == 0:
                            v_part(g, c)
                        if t >= 1:
                            p_part(g, t - 1, c)
                        if t < NT:
                            exponentials(g, t, c)
                    if g.na and t >= 1 and INNER[t - 1]:
                        p_part(g, t - 1, 2)
                    if g.project and t < NT:
                        piece_part(g, t)
                    if t >= 1:
                        output_half(g, t - 1)
                        if not g.project and t < NT:
                            take_mixed(g.l, t - 1)
                    if g.project and t == NT - 1:
                        k_hi_part(g)

            with act.Fori(0, DEPTH) as l:
                first = First(l)
                w_hi_part(l * CPL, 0, l * 2 * CPL)
                for i in range(NT):
                    act.wait_ge(norm_done, l * NT + i + 1)
                    act.activation(h_hi[:, i, :], normed[i % 2], ACT.Copy).then_inc(h_hi_done, 1)
                for t in range(NT):
                    if t % 2 == 0:
                        w_hi_part(first.chunk(t) + 1, (t // 2 + 1) % 2, first.piece(t))
                    piece_part(first, t)
                k_hi_part(first)
                groups(act, l, attend)
                take_mixed(l, NT - 1)
                for j in range(NT):
                    if j < NT - 1:
                        w_hi_part(l * CPL + 4 * GROUPS + j + 1, (j + 1) % 2, l * 2 * CPL + GROUPS * NT + 2 * j)
                    for hf in range(2):
                        n = l * 2 * CPL + GROUPS * NT + 2 * j + hf
                        act.wait_ge(piece_freed, n + 1)
                        square_of((l + 1) * 2 * NT + 2 * j + hf, j, hf)

        @block.tensor
        def _(pe):
            start_at_one(pe, pv_done, piece_done)

            def three(dst, a_hi, a_lo, b_hi, b_lo, start=True, stop=True):
                pe.matmul(dst, a_hi, b_hi, start=start, stop=False)
                pe.matmul(dst, a_hi, b_lo, start=False, stop=False)
                return pe.matmul(dst, a_lo, b_hi, start=False, stop=stop)

            def piece(n, chunk, t, ks):
                b, cols = (t // 2) % 2, slice((t % 2) * HALF, (t % 2 + 1) * HALF)
                if 0 in ks:
                    if not (isinstance(n, int) and n < 2):
                        pe.wait_ge(piece_freed, n - 1)
                    pe.wait_ge(w_lo_done, chunk + 1)
                for k in ks:
                    last = three(proj[:, t % 2], w_hi[:, b, k], w_lo[:, b, k], h_hi[:, k, cols], h_lo[:, k, cols],
                                 start=k == 0, stop=k == NT - 1)
                if NT - 1 in ks:
                    last.then_inc(piece_done, 1)

            def score(g, t):
                reached(pe, scores_read, 2 * g.step(t))
                if t == 0:
                    pe.wait_ge(q_ready, 2 * (g.group() + 1))
                    pe.wait_ge(k_ready, g.group() + 1)
                tile = slice(t * P, (t + 1) * P)
                first = KEY0[t] * W if g.na else 0
                spans = [(0, HALF), (HALF, WIDTH[t] if g.na else S)]
                for a, b in spans:
                    if a == b:
                        continue
                    for q, k, start in ((q_hi, k_hi, True), (q_hi, k_lo, False), (q_lo, k_hi, False)):
                        for m in range(2):
                            rows = slice(m * HD, (m + 1) * HD)
                            last = pe.matmul(scores[:, m, a:b], q[rows, tile], k[rows, first + a:first + b],
                                             start=start, stop=q is q_lo)
                last.then_inc(qk_done, 1)

            def turn_wait(g, *key):
                reached(pe, turn_freed, g.use(*key))

            def turn_v(g, c):
                turn_wait(g, "V", c)
                pe.wait_ge(piece_freed, g.l * 2 * CPL + g.g * NT + 2 * V_ + 2)
                for k in range(4):
                    last = pe.transpose(turn[:, k * P:(k + 1) * P], v_next[:, (4 * c + k) * P:(4 * c + k + 1) * P],
                                        ident[:])
                last.then_inc(turned, 1)

            def turn_p(g, t, c):
                turn_wait(g, "T", t, c)
                if g.na:
                    reached(pe, exp_done, 2 * g.step(t) + min(c, 1) + 1)
                else:
                    pe.wait_ge(comb_done, g.kind_step(t) + 1)
                if c == 2:
                    begin(pe, "pe")
                    for m in range(2):
                        last = pe.transpose(turn[0:HD, m * P:(m + 1) * P], prob[:, t % 2, m, HALF:HALF + HD], ident[:])
                else:
                    m, first = (c, 0) if g.na else (0, c * HALF)
                    for k in range(4):
                        last = pe.transpose(turn[:, k * P:(k + 1) * P],
                                            prob[:, t % 2, m, first + k * P:first + (k + 1) * P], ident[:])
                last.then_inc(turned, 1)

            def weigh(g, t):
                last_turn = ("T", t, 2 if g.na and INNER[t] else 1)
                reached(pe, turn_freed, g.use(*last_turn) + 1)
                reached(pe, u_done, g.step(t))
                if not g.na:
                    for k in range(NT):
                        at = slice((k % 4) * P, (k % 4 + 1) * P)
                        pe.matmul(mix[:, 0:2 * P], pt_hi[:, k // 4, at], v_hl[:, k, :], start=k == 0, stop=False)
                        last = pe.matmul(mix[:, 0:P], pt_lo[:, k // 4, at], v_hl[:, k, 0:P], start=False,
                                         stop=k == NT - 1)
                else:
                    for m in range(2):
                        k0, o = KEY0[t] // 2, m * P
                        for k in range(4):
                            at = slice(k * P, (k + 1) * P)
                            pe.matmul(mix[:, o:o + P], pt_hi[:, m, at], v_hl[:, k0 + k, o:o + P], start=k == 0,
                                      stop=False)
                            last = pe.matmul(mix[:, o:o + HD], pt_lo[:, m, at], v_hl[:, k0 + k, o:o + HD],
                                             start=False, stop=k == 3 and not INNER[t])
                        if INNER[t]:
                            pe.matmul(mix[:, o:o + P], px_hi[:, o:o + P], v_hl[0:HD, k0 + 4, o:o + P],
                                      start=False, stop=False)
                            last = pe.matmul(mix[:, o:o + HD], px_lo[:, o:o + P], v_hl[0:HD, k0 + 4, o:o + HD],
                                             start=False, stop=True)
                last.then_inc(pv_done, 1)

            def turn_u(g, t):
                turn_wait(g, "U", t)
                if g.na:
                    reached(pe, u_done, g.step(t) + 1)
                    src = u[:, t % 2, :]
                else:
                    pe.wait_ge(un_done, g.kind_step(t) + 1)
                    src = un[:, t % 2, :]
                pe.transpose(turn[:, 0:P], src, ident[:]).then_inc(turned, 1)

            def attend(g):
                for t in range(NT + 2):
                    front = t < NT
                    tail = 1 <= t <= NT
                    if front:
                        score(g, t)
                    parts = [range(0, 3), range(3, 6), range(6, 8)] if g.project and front else [(), (), ()]
                    if parts[0]:
                        piece(g.piece(t), g.chunk(t), t, parts[0])
                    if t == 0:
                        turn_v(g, 0)
                    if tail:
                        turn_p(g, t - 1, 0)
                    if parts[1]:
                        piece(g.piece(t), g.chunk(t), t, parts[1])
                    if t == 0:
                        turn_v(g, 1)
                    if tail:
                        turn_p(g, t - 1, 1)
                        if g.na and INNER[t - 1]:
                            turn_p(g, t - 1, 2)
                    if parts[2]:
                        piece(g.piece(t), g.chunk(t), t, parts[2])
                    if tail:
                        weigh(g, t - 1)
                    if t >= 2:
                        turn_u(g, t - 2)

            def norm(n):
                pe.wait_ge(sum_done, (n + 1) * 2 * NT)
                for i in range(NT):
                    last = pe.matmul(mix[:, i:i + 1], squares[:, i * P:(i + 1) * P], ones[:], start=True, stop=True)
                last.then_inc(stat_mm, 1)
                pe.wait_ge(rinv_done, n + 1)
                pe.wait_ge(made, MADE)
                for i in range(NT):
                    last = pe.matmul(scores[:, 0, i * P:(i + 1) * P], rinv[:, i:i + 1].to_broadcast([P, P]), ident[:],
                                     start=True, stop=True)
                last.then_inc(spread_mm, 1)

            with pe.Fori(0, DEPTH) as l:
                norm(l)
                first = First(l)
                pe.wait_ge(h_ready, l * 2 * NT + NT)
                for t in range(NT):
                    if t < 2:
                        piece(t, first.chunk(t), t, range(NT))
                    else:
                        piece(first.piece(t), first.chunk(t), t, range(NT))
                groups(pe, l, attend)
                pe.wait_ge(h_ready, (l + 1) * 2 * NT)
                for t in range(2 * NT):
                    piece(l * 2 * CPL + GROUPS * NT + t, l * CPL + 4 * GROUPS + t // 2, t, range(NT))
            norm(DEPTH)

        @block.vector
        def _(dve):
            start_at_one(dve, scores_read, turn_freed, u_done)
            dve.wait_ge(dist_int, 1)
            table = prob[:, 1].bitcast(I32).rearrange("p m s -> p (m s)")[:, 0:OFF + S]
            dve.scalar_tensor_tensor(dist[:], table, -1.0, table, ALU.mult, ALU.min).then_inc(consts_done, 1)
            dve.wait_ge(lam_loaded, 16)
            for l in range(DEPTH):
                for a in range(2):
                    dve.tensor_tensor_reduce(u[:, 0, 0:HD], lam_in[:, 2 * a, l], lam_in[:, 2 * a + 1, l], 1.0, 0.0,
                                             ALU.mult, ALU.add, lam_s[:, a, l:l + 1]).then_inc(lam_dot, 1)
                    dve.wait_ge(lam_dot, 2 * l + a + 1)
            dve.wait_ge(lam_exp, 1)
            dve.tensor_tensor(neglam[:], lam_e[:, 1], lam_e[:, 0], ALU.subtract).then_inc(consts_done, 1)
            dve.wait_ge(const_in, 48)
            dve.wait_ge(consts_done, 2)
            for l in range(DEPTH):
                dve.tensor_scalar(neglam[:, l:l + 1], neglam[:, l:l + 1], -LAM_INIT[l], None, ALU.add)\
                    .then_inc(consts_done, 1)
                dve.tensor_scalar(sgain[:, l:l + 1], sgain[:, l:l + 1], 1.0 - LAM_INIT[l], None, ALU.mult)\
                    .then_inc(consts_done, 1)
            dve.wait_ge(consts_done, CONSTS)

            def norm_stats(n):
                dve.wait_ge(stat_mm, n + 1)
                dve.tensor_scalar(stat[:], mix[:, 0:NT], 1.0 / D, EPS, ALU.mult, ALU.add).then_inc(stat_done, 1)
                dve.wait_ge(spread_mm, n + 1)

            def piece_part(g, t):
                ps, n, kind = proj[:, t % 2], g.piece(t), t // 2
                cols = slice((t % 2) * HALF, (t % 2 + 1) * HALF)
                halves = g.l * (4 * GROUPS) + (g.g + 1) * 4
                if kind == V_:
                    reached(dve, piece_done, n + 1)
                    dve.tensor_copy(v_next[:, cols], ps).then_inc(piece_freed, 1)
                if kind == K_:
                    reached(dve, piece_done, n + 1)
                    if not isinstance(g, First):
                        dve.wait_ge(k_ready, g.group() + 1)
                    dve.tensor_copy(k_next[:, cols], ps).then_inc(piece_freed, 1)
                if kind == G_:
                    m = g.l * (4 * GROUPS) + (g.g + 1) * 4 + 2 * (t % 2)
                    dve.wait_ge(piece_half, halves + t % 2 + 1)
                    dve.tensor_scalar(gate_exp[:], gate_exp[:], 1.0, None, ALU.add).then_inc(gate_step, 1)
                    dve.wait_ge(gate_step, m + 1)
                    dve.reciprocal(gate_exp[:], gate_exp[:]).then_inc(gate_step, 1)
                    dve.wait_ge(gate_step, m + 2)
                    if not isinstance(g, First):
                        dve.wait_ge(gate_ready, g.group() + 1)
                    dve.tensor_tensor(gate_next[:, cols], ps, gate_exp[:], ALU.mult).then_inc(piece_freed, 1)
                if kind == Q_:
                    dve.wait_ge(piece_half, halves + 2 + t % 2 + 1)
                    col = qscale[:, bass.ds(g.g + 1, 1)]
                    dve.scalar_tensor_tensor(q_lo[:, cols], ps, col, f32(q_hi[:, cols]), ALU.mult, ALU.subtract)\
                        .then_inc(q_ready, 1)
                    dve.wait_ge(q_ready, g.l * 2 * GROUPS + 2 * (g.g + 1) + t % 2 + 1)
                    dve.nop().then_inc(piece_freed, 1)

            def shifted(g, t, m):
                b, n = t % 2, 2 * g.step(t) + m
                if m == 0:
                    dve.wait_ge(qk_done, g.step(t) + 1)
                    begin(dve, "dve")
                w = WIDTH[t] if g.na else S
                if not g.na:
                    bias = dist[:, OFF - t * P:OFF - t * P + S]
                elif INNER[t]:
                    bias = inner[:, m, :]
                else:
                    first = (KEY0[t] - 2 * t + 6) * W
                    bias = edge[:, m, first:first + w]
                dve.tensor_tensor_reduce(prob[:, b, m, 0:w], scores[:, m, 0:w], bias, 1.0, -3e38, ALU.add, ALU.max,
                                         mx[:, b, m:m + 1]).then_inc(scores_read, 1)
                reached(dve, scores_read, n + 1)
                scale = -1.0 if g.na else nescale[:, bass.ds(g.i, 1)]
                dve.tensor_scalar(nm[:, b, m:m + 1], mx[:, b, m:m + 1], scale, None, ALU.mult).then_inc(shift_ready, 1)

            def turn_part(g, key, dst, src, hi):
                dve.wait_ge(turn_hi, g.split(*key) + 1)
                dve.tensor_tensor(dst, src, f32(hi), ALU.subtract).then_inc(turn_freed, 1)

            def v_part(g, c):
                tiles = v_hl[:, 4 * c:4 * c + 4]
                if g.na:
                    view = tiles.rearrange("p k (h s e) -> p k h s e", h=2, s=2)
                    hi, lo = view[:, :, :, 0, :], view[:, :, :, 1, :]
                    src = turn[:].rearrange("p (k h e) -> p k h e", k=4, h=2)
                else:
                    hi, lo, src = tiles[:, :, 0:P], tiles[:, :, P:2 * P], turn[:].rearrange("p (k e) -> p k e", k=4)
                turn_part(g, ("V", c), lo, src, hi)

            def p_part(g, t, c):
                if c == 2:
                    turn_part(g, ("T", t, c), px_lo[:], turn[0:HD, 0:256], px_hi[:])
                else:
                    turn_part(g, ("T", t, c), pt_lo[:, c, :], turn[:], pt_hi[:, c, :])

            def combine(g, t):
                b, n = t % 2, g.step(t)
                reached(dve, exp_done, 2 * n + 2)
                dve.reciprocal(rrec[:, b, :], rsum[:, b, :]).then_inc(rrec_done, 1)
                if not g.na:
                    k = g.kind_step(t)
                    dve.wait_ge(rrec_done, n + 1)
                    dve.scalar_tensor_tensor(cmix[:, b:b + 1], rrec[:, b, 1:2], neglam[:, bass.ds(g.l, 1)],
                                             rsum[:, b, 0:1], ALU.mult, ALU.mult).then_inc(cmix_done, 1)
                    dve.wait_ge(cmix_done, k + 1)
                    dve.scalar_tensor_tensor(prob[:, b, 0, :], prob[:, b, 1, :], cmix[:, b:b + 1], prob[:, b, 0, :],
                                             ALU.mult, ALU.add).then_inc(comb_done, 1)

            def output(g, t):
                b, n = t % 2, g.step(t)
                dve.wait_ge(u_half, n + 1)
                if g.na:
                    for m in range(2):
                        cols = slice(m * HD, (m + 1) * HD)
                        last = dve.scalar_tensor_tensor(u[:, b, cols], mix[:, m * P + HD:(m + 1) * P],
                                                        rrec[:, b, m:m + 1], u_hi[:, cols], ALU.mult, ALU.add)
                    last.then_inc(u_done, 1)
                else:
                    dve.scalar_tensor_tensor(u[:, b, :], mix[:, P:2 * P], rrec[:, b, 0:1], u_hi[:], ALU.mult, ALU.add)\
                        .then_inc(u_done, 1)

            def gated(g, t):
                cols = slice(t * P, (t + 1) * P)
                dve.wait_ge(turned, g.use("U", t) + 1)
                if t == 0:
                    dve.wait_ge(gate_ready, g.group() + 1)
                    reached(dve, mixed_out, 16 * g.group())
                if g.na:
                    dve.tensor_tensor(mixed[:, cols], turn[:, 0:P], gate[:, cols], ALU.mult).then_inc(turn_freed, 1)
                else:
                    dve.scalar_tensor_tensor(mixed[:, cols], turn[:, 0:P], sgain[:, bass.ds(g.l, 1)], gate[:, cols],
                                             ALU.mult, ALU.mult).then_inc(turn_freed, 1)

            def inner_bias(g):
                n = g.l * NA_G + g.i
                dve.wait_ge(edge_masked, n + 1)
                dve.tensor_copy(inner[:], edge[:, :, 2 * W:11 * W]).then_inc(inner_copied, 1)
                dve.wait_ge(inner_copied, n + 1)
                dve.memset(inner[0:W, :, 8 * W:9 * W], MASKED).then_inc(inner_ready, 1)
                dve.memset(inner[W:P, :, 0:W], MASKED).then_inc(inner_ready, 1)
                dve.wait_ge(inner_ready, 2 * n + 2)

            def take_mixed(l, i):
                dve.wait_ge(h_hi_done, l * 2 * NT + NT + i + 1)
                dve.tensor_tensor(h_lo[:, i, :], f32(h_lo[:, i, :]), f32(h_hi[:, i, :]), ALU.subtract)\
                    .then_inc(h_ready, 1)

            def attend(g):
                if g.na:
                    inner_bias(g)
                for t in range(NT + 2):
                    for c in range(2):
                        if t < NT:
                            shifted(g, t, c)
                        if t == 0:
                            v_part(g, c)
                        if 1 <= t <= NT:
                            p_part(g, t - 1, c)
                    if 1 <= t <= NT and g.na and INNER[t - 1]:
                        p_part(g, t - 1, 2)
                    if t < NT:
                        combine(g, t)
                    if g.project and t < NT:
                        piece_part(g, t)
                    if 1 <= t <= NT:
                        output(g, t - 1)
                        if not g.project and t < NT:
                            take_mixed(g.l, t - 1)
                    if t >= 2:
                        gated(g, t - 2)

            with dve.Fori(0, DEPTH) as l:
                norm_stats(l)
                for i in range(NT):
                    if i >= 2:
                        dve.wait_ge(h_ready, l * 2 * NT + i - 1)
                    dve.scalar_tensor_tensor(normed[i % 2], xt[:, i, :], ngain[:, bass.ds(l * NT + i, 1)],
                                             scores[:, 0, :], ALU.mult, ALU.mult).then_inc(norm_done, 1)
                    dve.wait_ge(h_hi_done, l * 2 * NT + i + 1)
                    dve.tensor_tensor(h_lo[:, i, :], normed[i % 2], f32(h_hi[:, i, :]), ALU.subtract)\
                        .then_inc(h_ready, 1)
                for t in range(NT):
                    piece_part(First(l), t)
                groups(dve, l, attend)
                take_mixed(l, NT - 1)
                for t in range(2 * NT):
                    n = l * 2 * CPL + GROUPS * NT + t
                    cols = slice((t % 2) * HALF, (t % 2 + 1) * HALF)
                    reached(dve, piece_done, n + 1)
                    dve.tensor_tensor(xt[:, t // 2, cols], xt[:, t // 2, cols], proj[:, t % 2], ALU.add)\
                        .then_inc(piece_freed, 1)
            norm_stats(DEPTH)
            for i in range(NT):
                if i >= 2:
                    dve.wait_ge(stored[i % 2], 16 * (i // 2))
                dve.scalar_tensor_tensor(normed[i % 2], xt[:, i, :], fgain[:, i:i + 1], scores[:, 0, :],
                                         ALU.mult, ALU.mult).then_inc(norm_done, 1)


def kernel(x, norm_g, w_in, w_out, lam_q1, lam_k1, lam_q2, lam_k2, subln_g, rpb, final_g):
    import concourse.bacc as bacc
    from concourse.bass_utils import run_bass_kernel_spmd

    f = lambda a: np.asarray(a)
    x, norm_g, w_in, w_out, subln_g, rpb, final_g = map(f, (x, norm_g, w_in, w_out, subln_g, rpb, final_g))
    depth, D, _ = w_in.shape
    S = x.shape[1]
    cut = lambda w: w.reshape(depth, D // P, P, -1, P).transpose(0, 3, 2, 1, 4)
    by_out = cut(w_in)
    q, k, v = [list(range(4 * j, 4 * j + 4)) + list(range(12 + 4 * j, 16 + 4 * j)) for j in range(3)]
    order = [c for g in range(8) for c in (v[g], k[g], 24 + g, q[g])]
    stream = np.concatenate([by_out[:, order], cut(w_out)], axis=1).reshape(-1, P, D)
    stream = np.concatenate([stream, stream[:1]])
    gap = np.zeros(64, rpb.dtype)
    columns = lambda a: np.ascontiguousarray(a.reshape(-1, P).T)
    arrays = {
        "x_t": x[0].T,
        "chunks": stream,
        "norm_gain": columns(norm_g),
        "final_gain": columns(final_g),
        "subln_gain": columns(subln_g),
        "lam_vecs": np.stack([f(lam_q1), f(lam_k1), f(lam_q2), f(lam_k2)])[None],
        "bias_rows": np.concatenate([gap, rpb.ravel(), gap]),
    }
    arrays = {n: np.ascontiguousarray(a) for n, a in arrays.items()}
    nc = bacc.Bacc("TRN2", target_bir_lowering=False, num_devices=1)
    aps = [nc.dram_tensor(n, a.shape, mybir.dt.from_np(a.dtype), kind="ExternalInput").ap() for n, a in arrays.items()]
    out = nc.dram_tensor("out_t", (D, S), F32, kind="ExternalOutput").ap()
    hybrid_encoder(nc, *aps, out)
    r = run_bass_kernel_spmd(nc, [arrays], core_ids=[0])
    return np.ascontiguousarray(r.results[0]["out_t"].T)[None]
```

```python
import numpy as np
import concourse.bass as bass
from concourse import mybir
from contextlib import ExitStack

ALU = mybir.AluOpType
ACT = mybir.ActivationFunctionType
F32 = mybir.dt.float32
F32R = mybir.dt.float32r
FP16 = mybir.dt.float16
I32 = mybir.dt.int32

P = 128
HALF = 512
MASKED = -1e30


def hybrid_encoder(nc, x_t, chunks, norm_gain, final_gain, subln_gain, lam_vecs, bias_rows, out_t):
    D, S = x_t.shape
    NT = D // P
    DEPTH = norm_gain.shape[1] // NT
    HD = lam_vecs.shape[3]
    DA_G, NA_G = 4, 4
    GROUPS = DA_G + NA_G
    RB = 2 * 16 - 1
    RR = 15
    W = 64
    CPL = 4 * GROUPS + NT
    EPS = 1e-6
    EDGE = 14
    LAM_INIT = [0.8 - 0.6 * float(np.exp(-0.3 * l)) for l in range(DEPTH)]
    SLOPES = [2.0 ** (-8.0 * (i + 1) / DA_G) for i in range(DA_G)]
    OFF = S - P
    MADE = 9
    CONSTS = 2 + 2 * DEPTH
    G_, V_, K_, Q_ = range(4)
    LEAD = 6

    KEY0 = [0, 0, 0, 2, 4, 6, 8, 8]
    INNER = [2 <= t <= 5 for t in range(NT)]
    WIDTH = [576 if INNER[t] else 512 for t in range(NT)]

    def uses(na):
        order, split = {}, {}
        def use(key, halves):
            order[key] = len(order)
            if halves:
                split[key] = len(split)
        for t in range(NT + 2):
            if t == 0:
                use(("V", 0), True)
                use(("V", 1), True)
            if 1 <= t <= NT:
                for c in range(3 if na and INNER[t - 1] else 2):
                    use(("T", t - 1, c), True)
            if t >= 2:
                use(("U", t - 2), False)
        return order, split
    ORDER = {na: uses(na)[0] for na in (False, True)}
    SPLIT = {na: uses(na)[1] for na in (False, True)}
    ORDERS = DA_G * len(ORDER[False]) + NA_G * len(ORDER[True])
    SPLITS = DA_G * len(SPLIT[False]) + NA_G * len(SPLIT[True])

    class Group:

        def __init__(self, l, na, i, project=True):
            self.l, self.na, self.i, self.project = l, na, i, project
            self.g = i + (DA_G if na else 0)

        def step(self, t):
            return self.l * (GROUPS * NT) + self.g * NT + t

        def kind_step(self, t):
            return self.l * (DA_G * NT) + self.i * NT + t

        def group(self):
            return self.l * GROUPS + self.g

        def use(self, *key):
            first = DA_G * len(ORDER[False]) if self.na else 0
            return self.l * ORDERS + first + self.i * len(ORDER[self.na]) + ORDER[self.na][key]

        def split(self, *key):
            first = DA_G * len(SPLIT[False]) if self.na else 0
            return self.l * SPLITS + first + self.i * len(SPLIT[self.na]) + SPLIT[self.na][key]

        def piece(self, t):
            return self.l * (2 * CPL) + LEAD + self.g * NT + t

        def chunk(self, t):
            return self.l * CPL + LEAD // 2 + self.g * 4 + t // 2

        def projects(self, t):
            return t < NT and (self.project or t // 2 == G_)

        def half(self, t):
            return self.l * (4 * GROUPS) + 2 + self.g * 4 + (2 if t // 2 == Q_ else 0) + t % 2

        def stores(self):
            return self.l * (GROUPS - 1) + self.g

    class First(Group):

        STEPS = range(NT - LEAD, NT)

        def __init__(self, l):
            self.l, self.na, self.i, self.g, self.project = l, False, -1, -1, True

    with ExitStack() as ctx:
        def sb(name, shape, dt=F32):
            return ctx.enter_context(nc.sbuf_tensor(name, shape, dt))

        def sem(name):
            return ctx.enter_context(nc.semaphore(name))

        xt = sb("xt", [P, NT, S])
        h_hi = sb("h_hi", [P, NT, S], F32R)
        h_lo = sb("h_lo", [P, NT, S], F32R)
        w_raw = sb("w_raw", [P, NT, P])
        w_hi = sb("w_hi", [P, 2, NT, P], F32R)
        w_lo = sb("w_lo", [P, 2, NT, P], F32R)
        q_hi = sb("q_hi", [P, S], F32R)
        q_lo = sb("q_lo", [P, S], F32R)
        k_hi = sb("k_hi", [P, S], F32R)
        k_lo = sb("k_lo", [P, S], F32R)
        k_next = sb("k_next", [P, S])
        v_next = sb("v_next", [P, S])
        v_hl = sb("v_hl", [P, NT, 256], F32R)
        gate = sb("gate", [P, S])
        gate_exp = sb("gate_exp", [P, S])
        prob = sb("prob", [P, 2, 2, S])
        pt_hi = sb("pt_hi", [P, 2, HALF], F32R)
        pt_lo = sb("pt_lo", [P, 2, HALF], F32R)
        px_hi = sb("px_hi", [HD, 256], F32R)
        px_lo = sb("px_lo", [HD, 256], F32R)
        dist = sb("dist", [P, OFF + S], FP16)
        edge = sb("edge", [P, 2, EDGE * W])
        inner = sb("inner", [P, 2, 9 * W])
        mixed = sb("mixed", [P, S])
        u_hi = sb("u_hi", [P, P])
        u = sb("u", [P, 2, P])
        un = sb("un", [P, 2, P])
        ident = sb("ident", [P, P])
        ones = sb("ones", [P, 1])
        colmask = sb("colmask", [P, W])
        ngain = sb("ngain", [P, DEPTH * NT])
        fgain = sb("fgain", [P, NT])
        sgain = sb("sgain", [P, DEPTH])
        qscale = sb("qscale", [P, GROUPS])
        escale = sb("escale", [P, DA_G])
        escale_now = sb("escale_now", [P, 1])
        nescale = sb("nescale", [P, DA_G])
        neglam = sb("neglam", [P, DEPTH])
        mx = sb("mx", [P, 2, 2])
        nm = sb("nm", [P, 2, 2])
        rsum = sb("rsum", [P, 2, 2])
        rrec = sb("rrec", [P, 2, 2])
        cmix = sb("cmix", [P, 2])
        ssq = sb("ssq", [P, 2])
        msq = sb("msq", [P, 2])
        rms = sb("rms", [P, 2])
        power = sb("power", [P, NT])
        stat = sb("stat", [P, NT])
        rinv = sb("rinv", [P, NT])
        lam_s = sb("lam_s", [P, 2, DEPTH])
        lam_e = sb("lam_e", [P, 2, DEPTH])
        squares = prob[:, 0, 0, :]
        square = prob[:, 0, 1, :]
        lam_in = gate[:, 0:4 * DEPTH * HD].rearrange("p (a l d) -> p a l d", a=4, l=DEPTH)
        normed = [prob[:, 1, 0, :], prob[:, 1, 1, :], square, squares]

        scores = ctx.enter_context(nc.psum_tensor("scores", [P, 2, S], F32))
        proj = ctx.enter_context(nc.psum_tensor("proj", [P, 2, HALF], F32))
        turn = ctx.enter_context(nc.psum_tensor("turn", [P, HALF], F32))
        mix = ctx.enter_context(nc.psum_tensor("mix", [P, HALF], F32))
        all_scores = scores[:].rearrange("p m s -> p (m s)")

        def turn_bank(na, key):
            return all_scores[:, 3 * HALF:] if na and ORDER[na][key] % 2 else turn[:]

        def window(t, m):
            return m * (3 * HALF - WIDTH[t])

        def bank(g, t):
            return scores[:, 1, (t % 2) * HALF:(t % 2 + 1) * HALF] if isinstance(g, First) and t // 2 == K_ else proj[:, t % 2]

        mixed_dram = nc.dram_tensor("mixed_dram", (D, S), F32).ap()
        bias_dram = nc.dram_tensor("bias_dram", (DEPTH * 2 * NA_G, 2, W, EDGE * W), F32).ap()

        x_in = [sem(f"x_in{i}") for i in range(NT)]
        const_in = sem("const_in")
        lam_loaded = sem("lam_loaded")
        bias_spread = sem("bias_spread")
        w_in = sem("w_in")
        edge_in = sem("edge_in")
        mixed_out = sem("mixed_out")
        mixed_in = [sem(f"mixed_in{i}") for i in range(NT)]
        stored = [sem(f"stored{b}") for b in range(len(normed))]
        made = sem("made")
        lam_dot = sem("lam_dot")
        lam_exp = sem("lam_exp")
        consts_done = sem("consts_done")
        dist_int = sem("dist_int")
        w_hi_done = sem("w_hi_done")
        w_lo_done = sem("w_lo_done")
        sq_done = sem("sq_done")
        sum_done = sem("sum_done")
        stat_mm = sem("stat_mm")
        stat_done = sem("stat_done")
        rinv_done = sem("rinv_done")
        spread_mm = sem("spread_mm")
        norm_done = sem("norm_done")
        h_hi_done = sem("h_hi_done")
        h_ready = sem("h_ready")
        h_ready_pool = sem("h_ready_pool")
        piece_done = sem("piece_done")
        piece_half = sem("piece_half")
        piece_freed = sem("piece_freed")
        gate_plus = sem("gate_plus")
        gate_rec = sem("gate_rec")
        gate_silu = sem("gate_silu")
        q_ready = sem("q_ready")
        k_hi_done = sem("k_hi_done")
        k_ready = sem("k_ready")
        edge_masked = sem("edge_masked")
        inner_copied = sem("inner_copied")
        inner_ready = sem("inner_ready")
        tail_done = sem("tail_done")
        qk_done = sem("qk_done")
        scores_read = sem("scores_read")
        shift_ready = sem("shift_ready")
        exp_done = sem("exp_done")
        escale_set = sem("escale_set")
        rrec_done = sem("rrec_done")
        cmix_done = sem("cmix_done")
        comb_done = sem("comb_done")
        turned = sem("turned")
        turn_hi = sem("turn_hi")
        turn_freed = sem("turn_freed")
        pv_done = sem("pv_done")
        u_half = sem("u_half")
        u_done = sem("u_done")
        ssq_done = sem("ssq_done")
        msq_done = sem("msq_done")
        rms_done = sem("rms_done")
        un_done = sem("un_done")

        f32 = lambda t: t.bitcast(F32)
        HR = NT // 2 + NT + 1
        TAKEN = {4: [0], 5: [1, 2], 6: [3], 7: [4, 5], 8: [6]}

        def norm_ready(e, l, k):
            if k % 2:
                e.wait_ge(h_ready_pool, l * (NT // 2) + k // 2 + 1)
            else:
                e.wait_ge(h_ready, l * HR + k // 2 + 1)

        def groups(e, l, attend):
            with e.Fori(0, DA_G) as i:
                attend(Group(l, False, i))
            with e.Fori(0, NA_G - 1) as i:
                attend(Group(l, True, i))
            attend(Group(l, True, NA_G - 1, project=False))

        begun = {e: sem(f"begun_{e}") for e in ("act", "dve", "pe", "pool")}

        def reached(e, count, n):
            e.wait_ge(count, n + 1)

        def start_at_one(e, *counts):
            for count in counts:
                e.sem_inc(count, 1)

        def begin(e, name):
            e.sem_inc(begun[name], 1)

        block = ctx.enter_context(nc.Block())

        @block.sync
        def _(sp):
            start_at_one(sp, mixed_out)
            for i in range(NT):
                sp.dma_start(xt[:, i, :], x_t[i * P:(i + 1) * P, :]).then_inc(x_in[i], 16)
                if i == 0:
                    sp.dma_start(w_raw[:], chunks[0].rearrange("p (t c) -> p t c", c=P)).then_inc(w_in, 16)
            sp.dma_start(ngain[:], norm_gain).then_inc(const_in, 16)
            sp.dma_start(fgain[:], final_gain).then_inc(const_in, 16)
            sp.dma_start(sgain[:], subln_gain).then_inc(const_in, 16)
            sp.dma_start(lam_in, bass.AP(lam_vecs.tensor, 0, [[0, P], [1, 4 * DEPTH * HD]])
                         .rearrange("p (a l d) -> p a l d", a=4, l=DEPTH)).then_inc(lam_loaded, 16)
            for h in range(DEPTH * 2 * NA_G):
                for odd in range(2):
                    first = W + (h * RR + 1 - odd) * RB + 15
                    sp.dma_start(bias_dram[h, odd].rearrange("q (r k) -> r q k", k=W),
                                 bass.AP(bias_rows.tensor, first, [[RB, EDGE], [-1, W], [1, W]]))\
                        .then_inc(bias_spread, 16)

            def load_chunk(c):
                sp.wait_ge(w_lo_done, c)
                sp.dma_start(w_raw[:], chunks[bass.ds(c, 1)].rearrange("o p (t c) -> (o p) t c", c=P))\
                    .then_inc(w_in, 16)

            def load_edge(l, i):
                for hd in range(2):
                    sp.dma_start(edge[:, hd, :], bias_dram[bass.ds(l * 2 * NA_G + 2 * i + hd, 1)]
                                 .rearrange("o r q k -> (o r q) k")).then_inc(edge_in, 16)

            def attend(g):
                for t in range(0, NT, 2):
                    if g.projects(t):
                        load_chunk(g.chunk(t) + 1)
                if g.project:
                    if g.na:
                        reached(sp, scores_read, 2 * g.step(NT))
                        load_edge(g.l, g.i + 1)
                else:
                    reached(sp, piece_done, g.l * 2 * CPL + GROUPS * NT)
                    reached(sp, mixed_out, 16 * g.stores())
                    for i in range(NT - 1):
                        sp.dma_start(f32(h_lo[:, i, :]), mixed_dram[i * P:(i + 1) * P, :])\
                            .then_inc(mixed_in[i], 16)
                if g.project:
                    reached(sp, turn_freed, g.use("U", NT - 1) + 1)
                    sp.dma_start(mixed_dram[bass.ds(g.g * P, P), :], mixed[:]).then_inc(mixed_out, 16)

            with sp.Fori(0, DEPTH) as l:
                sp.wait_ge(bias_spread, 16 * DEPTH * 4 * NA_G)
                reached(sp, scores_read, 2 * l * GROUPS * NT)
                load_edge(l, 0)
                for t in First.STEPS[::2]:
                    load_chunk(First(l).chunk(t) + 1)
                groups(sp, l, attend)
                for j in range(NT - 1):
                    load_chunk(l * CPL + 4 * GROUPS + j + 1)
                sp.wait_ge(w_lo_done, (l + 1) * CPL)
                sp.dma_start(w_raw[:], chunks[bass.ds((l + 1) * CPL, 1)].rearrange("o p (t c) -> (o p) t c", c=P))\
                    .then_inc(w_in, 16)
            for i in range(NT):
                sp.wait_ge(norm_done, DEPTH * NT + i + 1)
                sp.dma_start(out_t[i * P:(i + 1) * P, :], normed[i % 4]).then_inc(stored[i % 4], 16)
            for b in range(4):
                sp.wait_ge(stored[b], 16 * NT // 4)
            sp.wait_ge(w_in, 16 * (DEPTH * CPL + 1))
            sp.wait_ge(const_in, 48)

        @block.gpsimd
        def _(pool):
            pool.memset(ident[:], 0.0).then_inc(made, 1)
            pool.memset(colmask[:], 0.0).then_inc(made, 1)
            pool.memset(ones[:], 1.0).then_inc(made, 1)
            pool.memset(power[:], -0.5).then_inc(made, 1)
            for i in range(DA_G):
                pool.memset(qscale[:, i:i + 1], HD ** -0.5 / SLOPES[i])
                pool.memset(escale[:, i:i + 1], SLOPES[i])
                pool.memset(nescale[:, i:i + 1], -SLOPES[i])
            pool.memset(qscale[:, DA_G:], HD ** -0.5)
            table = prob[:, 1].bitcast(I32).rearrange("p m s -> p (m s)")[:, 0:OFF + S]
            pool.iota(table, pattern=[[1, OFF + S]], base=-OFF, channel_multiplier=-1).then_inc(dist_int, 1)
            pool.wait_ge(made, 4)
            pool.affine_select(out=ident[:], in_=ident[:], compare_op=ALU.not_equal, fill=1.0, base=0,
                               pattern=[[-1, P]], channel_multiplier=1).then_inc(made, 1)
            n = 5
            for first, base, sign in ((0, 8, 1), (16, 7 - 16, -1)):
                for r in range(2):
                    part = colmask[r * W:(r + 1) * W, first:first + 48]
                    pool.wait_ge(made, n)
                    pool.affine_select(out=part, in_=part, compare_op=ALU.is_ge, fill=MASKED, base=base,
                                       pattern=[[sign, 48]], channel_multiplier=-sign).then_inc(made, 1)
                    n += 1
            pool.wait_ge(made, MADE)

            def w_lo_part(c, b):
                pool.wait_ge(w_hi_done, c + 1)
                pool.tensor_tensor(w_lo[:, b], w_raw[:], f32(w_hi[:, b]), ALU.subtract).then_inc(w_lo_done, 1)

            def mask_edge(l, i):
                pool.wait_ge(edge_in, 32 * (l * NA_G + i + 1))
                pool.wait_ge(made, MADE)
                rows = edge[:].rearrange("p h (r k) -> p (h r) k", k=W)
                pool.tensor_tensor(rows, rows, colmask[:].unsqueeze(1).to_broadcast([P, 2 * EDGE, W]), ALU.add)\
                    .then_inc(edge_masked, 1)

            def k_lo_part(n):
                pool.wait_ge(k_hi_done, n + 1)
                pool.tensor_tensor(k_lo[:], k_next[:], f32(k_hi[:]), ALU.subtract).then_inc(k_ready, 1)

            def normalise(g, t):
                b, n = t % 2, g.kind_step(t)
                pool.wait_ge(ssq_done, n + 1)
                begin(pool, "pool")
                pool.tensor_scalar(msq[:, b:b + 1], ssq[:, b:b + 1], 1.0 / P, EPS, ALU.mult, ALU.add)\
                    .then_inc(msq_done, 1)
                pool.wait_ge(msq_done, n + 1)
                pool.tensor_tensor(rms[:, b:b + 1], msq[:, b:b + 1], power[:, 0:1], ALU.pow).then_inc(rms_done, 1)
                pool.wait_ge(rms_done, n + 1)
                begin(pool, "pool")
                pool.tensor_scalar(un[:, b, :], u[:, b, :], rms[:, b:b + 1], None, ALU.mult).then_inc(un_done, 1)

            def attend(g):
                for t in range(NT + 1):
                    if g.projects(t) and t % 2 == 0:
                        w_lo_part(g.chunk(t) + 1, (t // 2) % 2)
                    if not g.na and t >= 1:
                        normalise(g, t - 1)
                    if g.project and t == NT - 1:
                        k_lo_part(g.group() + 1)
                if g.na and g.project:
                    mask_edge(g.l, g.i + 1)

            def norm_stats(n):
                pool.wait_ge(stat_done, n + 1)
                pool.tensor_tensor(rinv[:], stat[:], power[:], ALU.pow).then_inc(rinv_done, 1)

            def add_square(n, cols):
                pool.wait_ge(sq_done, n + 1)
                pool.tensor_tensor(squares[:, cols], squares[:, cols], square[:, cols], ALU.add)\
                    .then_inc(sum_done, 1)

            for i in range(NT):
                for hf in range(2):
                    cols = slice(hf * HALF, (hf + 1) * HALF)
                    if i == 0:
                        pool.wait_ge(sq_done, hf + 1)
                        pool.nop().then_inc(sum_done, 1)
                    else:
                        add_square(2 * i + hf, cols)
            with pool.Fori(0, DEPTH) as l:
                w_lo_part(l * CPL, 0)
                first = First(l)
                w_lo_part(first.chunk(2) + 1, 1)
                norm_stats(l)
                for i in range(1, NT, 2):
                    pool.wait_ge(h_hi_done, l * (2 * NT + 1) + i + 1)
                    pool.tensor_tensor(h_lo[:, i, :], normed[i % 4], f32(h_hi[:, i, :]), ALU.subtract)\
                        .then_inc(h_ready_pool, 1)
                for t in First.STEPS[2::2]:
                    w_lo_part(first.chunk(t) + 1, (t // 2) % 2)
                k_lo_part(l * GROUPS)
                mask_edge(l, 0)
                groups(pool, l, attend)
                for j in range(NT):
                    if j < NT - 1:
                        w_lo_part(l * CPL + 4 * GROUPS + j + 1, (j + 1) % 2)
                    for hf in range(2):
                        cols = slice(hf * HALF, (hf + 1) * HALF)
                        n = (l + 1) * 2 * NT + 2 * j + hf
                        if j == 0:
                            pool.wait_ge(sq_done, n + 1)
                            pool.nop().then_inc(sum_done, 1)
                        else:
                            add_square(n, cols)
            norm_stats(DEPTH)

        @block.scalar
        def _(act):
            start_at_one(act, exp_done)

            def square_of(n, i, hf):
                cols = slice(hf * HALF, (hf + 1) * HALF)
                dst = squares if i == 0 else square
                if i > 0:
                    act.wait_ge(sum_done, n - 1)
                act.activation(dst[:, cols], xt[:, i, cols], ACT.Square).then_inc(sq_done, 1)

            for i in range(NT):
                act.wait_ge(x_in[i], 16)
                for hf in range(2):
                    square_of(2 * i + hf, i, hf)
            act.wait_ge(lam_dot, 2 * DEPTH)
            act.activation(lam_e[:], lam_s[:], ACT.Exp).then_inc(lam_exp, 1)

            def w_hi_part(c, b, freed):
                act.wait_ge(w_in, 16 * (c + 1))
                reached(act, piece_done, freed)
                act.activation(w_hi[:, b], w_raw[:], ACT.Copy).then_inc(w_hi_done, 1)

            def piece_part(g, t):
                ps, n, kind = bank(g, t), g.piece(t), t // 2
                cols = slice((t % 2) * HALF, (t % 2 + 1) * HALF)
                if kind == G_:
                    reached(act, piece_done, n + 1)
                    if t == 0:
                        reached(act, turn_freed, g.use("V", 0))
                    act.activation(gate_exp[:, cols], ps, ACT.Exp, scale=-1.0).then_inc(piece_half, 1)
                if kind == Q_:
                    reached(act, piece_done, n + 1)
                    act.wait_ge(qk_done, g.step(NT))
                    col = qscale[:, bass.ds(g.g + 1, 1)]
                    begin(act, "act")
                    act.activation(q_hi[:, cols], ps, ACT.Copy, scale=col).then_inc(piece_half, 1)

            def k_hi_part(g):
                act.wait_ge(qk_done, g.step(NT))
                act.wait_ge(piece_freed, g.piece(2 * K_ + 1) + 1)
                act.activation(k_hi[:], k_next[:], ACT.Copy).then_inc(k_hi_done, 1)

            def turn_part(g, key, dst, src):
                act.wait_ge(turned, g.use(*key) + 1)
                act.activation(dst, src, ACT.Copy).then_inc(turn_hi, 1)

            def v_part(g, c):
                src = turn_bank(g.na, ("V", c))
                if g.na:
                    dst = v_hl[:, 4 * c:4 * c + 4].rearrange("p k (h s e) -> p k h s e", h=2, s=2)[:, :, :, 0, :]
                    src = src.rearrange("p (k h e) -> p k h e", k=4, h=2)
                else:
                    dst, src = v_hl[:, 4 * c:4 * c + 4, 0:P], src.rearrange("p (k e) -> p k e", k=4)
                turn_part(g, ("V", c), dst, src)

            def p_part(g, t, c):
                reached(act, pv_done, g.step(t))
                src = turn_bank(g.na, ("T", t, c))
                if c == 2:
                    turn_part(g, ("T", t, c), px_hi[:], src[0:HD, 0:256])
                else:
                    turn_part(g, ("T", t, c), pt_hi[:, c, :], src)

            def exponentials(g, t, m):
                b = t % 2
                act.wait_ge(shift_ready, 2 * g.step(t) + m + 1)
                s = prob[:, b, m, 0:WIDTH[t] if g.na else S]
                scale = 1.0 if g.na else escale_now[:]
                act.activation(s, s, ACT.Exp, bias=nm[:, b, m:m + 1], scale=scale,
                               accum_out=rsum[:, b, m:m + 1]).then_inc(exp_done, 1)

            def output_half(g, t):
                b, n = t % 2, g.step(t)
                reached(act, pv_done, n + 1)
                act.wait_ge(rrec_done, n + 1)
                reached(act, u_done, n)
                if g.na:
                    for m in range(2):
                        last = act.activation(u_hi[:, m * HD:(m + 1) * HD], mix[:, m * P:m * P + HD], ACT.Copy,
                                              scale=rrec[:, b, m:m + 1])
                    last.then_inc(u_half, 1)
                else:
                    act.activation(u_hi[:], mix[:, 0:P], ACT.Copy, scale=rrec[:, b, 0:1]).then_inc(u_half, 1)
                    reached(act, u_done, n + 1)
                    act.activation(u_hi[:], u[:, b, :], ACT.Square, accum_out=ssq[:, b:b + 1]).then_inc(ssq_done, 1)

            def take_mixed(l, i):
                act.wait_ge(mixed_in[i], 16 * (l + 1))
                act.activation(h_hi[:, i, :], f32(h_lo[:, i, :]), ACT.Copy).then_inc(h_hi_done, 1)

            def attend(g):
                if not g.na:
                    n = g.l * DA_G + g.i
                    reached(act, exp_done, 2 * g.step(0))
                    act.activation(escale_now[:], escale[:, bass.ds(g.i, 1)], ACT.Copy).then_inc(escale_set, 1)
                    act.wait_ge(escale_set, n + 1)
                for t in range(NT + 1):
                    if g.projects(t) and t % 2 == 0:
                        w_hi_part(g.chunk(t) + 1, (t // 2) % 2, g.piece(t))
                    for c in range(2):
                        if t == 0:
                            v_part(g, c)
                        if t >= 1:
                            p_part(g, t - 1, c)
                        if t < NT:
                            exponentials(g, t, c)
                    if g.na and t >= 1 and INNER[t - 1]:
                        p_part(g, t - 1, 2)
                    if g.projects(t):
                        piece_part(g, t)
                    if t >= 1:
                        output_half(g, t - 1)
                    if not g.project:
                        for i in TAKEN.get(t, ()):
                            take_mixed(g.l, i)
                    if g.project and t == NT - 1:
                        k_hi_part(g)

            with act.Fori(0, DEPTH) as l:
                first = First(l)
                w_hi_part(l * CPL, 0, l * 2 * CPL)
                w_hi_part(l * CPL + 1, 1, l * 2 * CPL)
                for i in range(NT):
                    act.wait_ge(norm_done, l * NT + i + 1)
                    act.activation(h_hi[:, i, :], normed[i % 4], ACT.Copy).then_inc(h_hi_done, 1)
                for t in First.STEPS:
                    if t % 2 == 0 and t > 2:
                        w_hi_part(first.chunk(t) + 1, (t // 2) % 2, first.piece(t))
                    piece_part(first, t)
                k_hi_part(first)
                groups(act, l, attend)
                reached(act, turn_freed, Group(l, True, NA_G - 1).use("U", NT - 1) + 1)
                for hf in range(2):
                    cols = slice(hf * HALF, (hf + 1) * HALF)
                    act.activation(h_hi[:, NT - 1, cols], mixed[:, cols], ACT.Copy).then_inc(h_hi_done, 1)
                for j in range(NT):
                    if j < NT - 1:
                        w_hi_part(l * CPL + 4 * GROUPS + j + 1, (j + 1) % 2, l * 2 * CPL + GROUPS * NT + 2 * j)
                    for hf in range(2):
                        n = l * 2 * CPL + GROUPS * NT + 2 * j + hf
                        act.wait_ge(piece_freed, n + 1)
                        square_of((l + 1) * 2 * NT + 2 * j + hf, j, hf)

        @block.tensor
        def _(pe):
            start_at_one(pe, pv_done, piece_done)

            def three(dst, a_hi, a_lo, b_hi, b_lo, start=True, stop=True):
                pe.matmul(dst, a_hi, b_hi, start=start, stop=False)
                pe.matmul(dst, a_hi, b_lo, start=False, stop=False)
                return pe.matmul(dst, a_lo, b_hi, start=False, stop=stop)

            def piece(dst, n, chunk, b, t, ks, ready=None):
                cols = slice((t % 2) * HALF, (t % 2 + 1) * HALF)
                if 0 in ks:
                    if n is not None:
                        pe.wait_ge(piece_freed, n - 1)
                    pe.wait_ge(w_lo_done, chunk + 1)
                for k in ks:
                    if ready:
                        ready(k)
                    last = three(dst, w_hi[:, b, k], w_lo[:, b, k], h_hi[:, k, cols], h_lo[:, k, cols],
                                 start=k == 0, stop=k == NT - 1)
                if NT - 1 in ks:
                    last.then_inc(piece_done, 1)

            def group_piece(g, t, ks):
                piece(bank(g, t), g.piece(t), g.chunk(t), (t // 2 + 1) % 2, t, ks)

            def score(g, t):
                reached(pe, scores_read, 2 * g.step(t))
                if t == 0:
                    pe.wait_ge(q_ready, 2 * (g.group() + 1))
                    pe.wait_ge(k_ready, g.group() + 1)
                tile = slice(t * P, (t + 1) * P)
                first = KEY0[t] * W if g.na else 0
                products = ((q_hi, k_hi), (q_hi, k_lo), (q_lo, k_hi))

                def product(m, p, at, a, b):
                    rows = slice(m * HD, (m + 1) * HD)
                    q, k = products[p]
                    return pe.matmul(all_scores[:, at + a:at + b], q[rows, tile], k[rows, first + a:first + b],
                                     start=p == 0, stop=p == 2)

                at = [window(t, m) if g.na else m * S for m in range(2)]
                spans = [[(0, HALF)], [(WIDTH[t] - HALF, WIDTH[t])]] if g.na else [[(0, HALF), (HALF, S)]] * 2
                def tail(m, a, b):
                    for p in range(3):
                        last = product(m, p, at[m], a, b)
                    return last

                wide = g.na and INNER[t]
                if wide:
                    tail(0, HALF, WIDTH[t]).then_inc(tail_done, 1)
                for pair in zip(*spans):
                    for p in range(3):
                        for m in range(2):
                            last = product(m, p, at[m], *pair[m])
                if wide:
                    pe.wait_ge(tail_done, (g.l * NA_G + g.i) * sum(INNER) + sum(INNER[:t]) + 1)
                    last = tail(1, 0, WIDTH[t] - HALF)
                last.then_inc(qk_done, 1)

            def turn_wait(g, *key):
                reached(pe, turn_freed, g.use(*key) - (1 if g.na and key != ("V", 0) else 0))
                return turn_bank(g.na, key)

            def turn_v(g, c):
                dst = turn_wait(g, "V", c)
                pe.wait_ge(piece_freed, g.piece(2 * V_) - NT + 2)
                for k in range(4):
                    last = pe.transpose(dst[:, k * P:(k + 1) * P], v_next[:, (4 * c + k) * P:(4 * c + k + 1) * P],
                                        ident[:])
                last.then_inc(turned, 1)

            def turn_p(g, t, c):
                dst = turn_wait(g, "T", t, c)
                if g.na:
                    reached(pe, exp_done, 2 * g.step(t) + min(c, 1) + 1)
                else:
                    pe.wait_ge(comb_done, g.kind_step(t) + 1)
                if c == 2:
                    begin(pe, "pe")
                    for m in range(2):
                        last = pe.transpose(dst[0:HD, m * P:(m + 1) * P], prob[:, t % 2, m, HALF:HALF + HD], ident[:])
                else:
                    m, first = (c, 0) if g.na else (0, c * HALF)
                    for k in range(4):
                        last = pe.transpose(dst[:, k * P:(k + 1) * P],
                                            prob[:, t % 2, m, first + k * P:first + (k + 1) * P], ident[:])
                last.then_inc(turned, 1)

            def weigh(g, t):
                last_turn = ("T", t, 2 if g.na and INNER[t] else 1)
                reached(pe, turn_freed, g.use(*last_turn) + 1)
                reached(pe, u_done, g.step(t))
                if not g.na:
                    for k in range(NT):
                        at = slice((k % 4) * P, (k % 4 + 1) * P)
                        pe.matmul(mix[:, 0:2 * P], pt_hi[:, k // 4, at], v_hl[:, k, :], start=k == 0, stop=False)
                        last = pe.matmul(mix[:, 0:P], pt_lo[:, k // 4, at], v_hl[:, k, 0:P], start=False,
                                         stop=k == NT - 1)
                else:
                    for m in range(2):
                        k0, o = KEY0[t] // 2, m * P
                        for k in range(4):
                            at = slice(k * P, (k + 1) * P)
                            pe.matmul(mix[:, o:o + P], pt_hi[:, m, at], v_hl[:, k0 + k, o:o + P], start=k == 0,
                                      stop=False)
                            last = pe.matmul(mix[:, o:o + HD], pt_lo[:, m, at], v_hl[:, k0 + k, o:o + HD],
                                             start=False, stop=k == 3 and not INNER[t])
                        if INNER[t]:
                            pe.matmul(mix[:, o:o + P], px_hi[:, o:o + P], v_hl[0:HD, k0 + 4, o:o + P],
                                      start=False, stop=False)
                            last = pe.matmul(mix[:, o:o + HD], px_lo[:, o:o + P], v_hl[0:HD, k0 + 4, o:o + HD],
                                             start=False, stop=True)
                last.then_inc(pv_done, 1)

            def turn_u(g, t):
                dst = turn_wait(g, "U", t)
                if g.na:
                    reached(pe, u_done, g.step(t) + 1)
                    src = u[:, t % 2, :]
                else:
                    pe.wait_ge(un_done, g.kind_step(t) + 1)
                    src = un[:, t % 2, :]
                pe.transpose(dst[:, 0:P], src, ident[:]).then_inc(turned, 1)

            def attend(g):
                for t in range(NT + 2):
                    front = t < NT
                    tail = 1 <= t <= NT
                    if front:
                        score(g, t)
                    parts = [range(0, 3), range(3, 6), range(6, 8)] if g.projects(t) else [(), (), ()]
                    if parts[0]:
                        group_piece(g, t, parts[0])
                    if t == 0:
                        turn_v(g, 0)
                    if tail:
                        turn_p(g, t - 1, 0)
                    if parts[1]:
                        group_piece(g, t, parts[1])
                    if t == 0:
                        turn_v(g, 1)
                    if tail:
                        turn_p(g, t - 1, 1)
                        if g.na and INNER[t - 1]:
                            turn_p(g, t - 1, 2)
                    if parts[2]:
                        group_piece(g, t, parts[2])
                    if tail:
                        weigh(g, t - 1)
                    if t >= 2:
                        turn_u(g, t - 2)

            def norm(n):
                pe.wait_ge(sum_done, (n + 1) * 2 * NT)
                for i in range(NT):
                    last = pe.matmul(mix[:, i:i + 1], squares[:, i * P:(i + 1) * P], ones[:], start=True, stop=True)
                last.then_inc(stat_mm, 1)
                pe.wait_ge(rinv_done, n + 1)
                pe.wait_ge(made, MADE)
                for i in range(NT):
                    last = pe.matmul(scores[:, 0, i * P:(i + 1) * P], rinv[:, i:i + 1].to_broadcast([P, P]), ident[:],
                                     start=True, stop=True)
                last.then_inc(spread_mm, 1)

            with pe.Fori(0, DEPTH) as l:
                norm(l)
                first = First(l)
                for j in range(2):
                    pe.wait_ge(w_lo_done, l * CPL + j + 1)
                for k in range(NT):
                    norm_ready(pe, l, k)
                    for t in First.STEPS[:4]:
                        b, cols = (t // 2 + 1) % 2, slice((t % 2) * HALF, (t % 2 + 1) * HALF)
                        last = three(bank(first, t), w_hi[:, b, k], w_lo[:, b, k], h_hi[:, k, cols],
                                     h_lo[:, k, cols], start=k == 0, stop=k == NT - 1)
                        if k == NT - 1:
                            last.then_inc(piece_done, 1)
                for t in First.STEPS[4:]:
                    group_piece(first, t, range(NT))
                groups(pe, l, attend)
                mixed_ready = l * HR + NT // 2

                def out_piece(t, ks):
                    piece(proj[:, t % 2], l * 2 * CPL + GROUPS * NT + t, l * CPL + 4 * GROUPS + t // 2, (t // 2) % 2,
                          t, ks)

                pe.wait_ge(h_ready, mixed_ready + NT - 1)
                for t in range(2):
                    out_piece(t, range(NT - 1))
                for t in range(2):
                    pe.wait_ge(h_ready, mixed_ready + NT + t)
                    out_piece(t, [NT - 1])
                for t in range(2, 2 * NT):
                    out_piece(t, range(NT))
            norm(DEPTH)

        @block.vector
        def _(dve):
            start_at_one(dve, scores_read, turn_freed, u_done)
            dve.wait_ge(dist_int, 1)
            table = prob[:, 1].bitcast(I32).rearrange("p m s -> p (m s)")[:, 0:OFF + S]
            dve.scalar_tensor_tensor(dist[:], table, -1.0, table, ALU.mult, ALU.min).then_inc(consts_done, 1)
            dve.wait_ge(lam_loaded, 16)
            for l in range(DEPTH):
                for a in range(2):
                    dve.tensor_tensor_reduce(u[:, 0, 0:HD], lam_in[:, 2 * a, l], lam_in[:, 2 * a + 1, l], 1.0, 0.0,
                                             ALU.mult, ALU.add, lam_s[:, a, l:l + 1]).then_inc(lam_dot, 1)
                    dve.wait_ge(lam_dot, 2 * l + a + 1)
            dve.wait_ge(lam_exp, 1)
            dve.tensor_tensor(neglam[:], lam_e[:, 1], lam_e[:, 0], ALU.subtract).then_inc(consts_done, 1)
            dve.wait_ge(const_in, 48)
            dve.wait_ge(consts_done, 2)
            for l in range(DEPTH):
                dve.tensor_scalar(neglam[:, l:l + 1], neglam[:, l:l + 1], -LAM_INIT[l], None, ALU.add)\
                    .then_inc(consts_done, 1)
                dve.tensor_scalar(sgain[:, l:l + 1], sgain[:, l:l + 1], 1.0 - LAM_INIT[l], None, ALU.mult)\
                    .then_inc(consts_done, 1)
            dve.wait_ge(consts_done, CONSTS)

            def norm_stats(n):
                dve.wait_ge(stat_mm, n + 1)
                dve.tensor_scalar(stat[:], mix[:, 0:NT], 1.0 / D, EPS, ALU.mult, ALU.add).then_inc(stat_done, 1)
                dve.wait_ge(spread_mm, n + 1)

            def piece_part(g, t):
                ps, n, kind = bank(g, t), g.piece(t), t // 2
                cols = slice((t % 2) * HALF, (t % 2 + 1) * HALF)
                if kind == V_:
                    reached(dve, piece_done, n + 1)
                    dve.tensor_copy(v_next[:, cols], ps).then_inc(piece_freed, 1)
                if kind == K_:
                    reached(dve, piece_done, n + 1)
                    if not isinstance(g, First):
                        dve.wait_ge(k_ready, g.group() + 1)
                    dve.tensor_copy(k_next[:, cols], ps).then_inc(piece_freed, 1)
                if kind == G_:
                    dve.wait_ge(piece_half, g.half(t) + 1)
                    dve.tensor_copy(gate[:, cols], ps).then_inc(piece_freed, 1)
                    dve.tensor_scalar(gate_exp[:, cols], gate_exp[:, cols], 1.0, None, ALU.add).then_inc(gate_plus, 1)
                if kind == Q_:
                    dve.wait_ge(piece_half, g.half(t) + 1)
                    col = qscale[:, bass.ds(g.g + 1, 1)]
                    dve.scalar_tensor_tensor(q_lo[:, cols], ps, col, f32(q_hi[:, cols]), ALU.mult, ALU.subtract)\
                        .then_inc(q_ready, 1)
                    dve.wait_ge(q_ready, g.l * 2 * GROUPS + 2 * (g.g + 1) + t % 2 + 1)
                    dve.nop().then_inc(piece_freed, 1)

            def silu(g, t):
                cols = slice(t * P, (t + 1) * P)
                if t % 4 == 0:
                    dve.wait_ge(gate_plus, 2 * g.group() + t // 4 + 1)
                    dve.wait_ge(piece_freed, g.piece(t // 4) + 1)
                dve.reciprocal(gate_exp[:, cols], gate_exp[:, cols]).then_inc(gate_rec, 1)
                dve.wait_ge(gate_rec, g.step(t) + 1)
                dve.tensor_tensor(gate[:, cols], gate[:, cols], gate_exp[:, cols], ALU.mult).then_inc(gate_silu, 1)

            def shifted(g, t, m):
                b, n = t % 2, 2 * g.step(t) + m
                if m == 0:
                    dve.wait_ge(qk_done, g.step(t) + 1)
                    begin(dve, "dve")
                w = WIDTH[t] if g.na else S
                if not g.na:
                    bias = dist[:, OFF - t * P:OFF - t * P + S]
                elif INNER[t]:
                    bias = inner[:, m, :]
                else:
                    first = (KEY0[t] - 2 * t + 6) * W
                    bias = edge[:, m, first:first + w]
                at = window(t, m) if g.na else m * S
                dve.tensor_tensor_reduce(prob[:, b, m, 0:w], all_scores[:, at:at + w], bias, 1.0, -3e38, ALU.add, ALU.max,
                                         mx[:, b, m:m + 1]).then_inc(scores_read, 1)
                reached(dve, scores_read, n + 1)
                scale = -1.0 if g.na else nescale[:, bass.ds(g.i, 1)]
                dve.tensor_scalar(nm[:, b, m:m + 1], mx[:, b, m:m + 1], scale, None, ALU.mult).then_inc(shift_ready, 1)

            def turn_part(g, key, dst, src, hi):
                dve.wait_ge(turn_hi, g.split(*key) + 1)
                dve.tensor_tensor(dst, src, f32(hi), ALU.subtract).then_inc(turn_freed, 1)

            def v_part(g, c):
                tiles, src = v_hl[:, 4 * c:4 * c + 4], turn_bank(g.na, ("V", c))
                if g.na:
                    view = tiles.rearrange("p k (h s e) -> p k h s e", h=2, s=2)
                    hi, lo = view[:, :, :, 0, :], view[:, :, :, 1, :]
                    src = src.rearrange("p (k h e) -> p k h e", k=4, h=2)
                else:
                    hi, lo, src = tiles[:, :, 0:P], tiles[:, :, P:2 * P], src.rearrange("p (k e) -> p k e", k=4)
                turn_part(g, ("V", c), lo, src, hi)

            def p_part(g, t, c):
                src = turn_bank(g.na, ("T", t, c))
                if c == 2:
                    turn_part(g, ("T", t, c), px_lo[:], src[0:HD, 0:256], px_hi[:])
                else:
                    turn_part(g, ("T", t, c), pt_lo[:, c, :], src, pt_hi[:, c, :])

            def combine(g, t):
                b, n = t % 2, g.step(t)
                reached(dve, exp_done, 2 * n + 2)
                dve.reciprocal(rrec[:, b, :], rsum[:, b, :]).then_inc(rrec_done, 1)
                if not g.na:
                    k = g.kind_step(t)
                    dve.wait_ge(rrec_done, n + 1)
                    dve.scalar_tensor_tensor(cmix[:, b:b + 1], rrec[:, b, 1:2], neglam[:, bass.ds(g.l, 1)],
                                             rsum[:, b, 0:1], ALU.mult, ALU.mult).then_inc(cmix_done, 1)
                    dve.wait_ge(cmix_done, k + 1)
                    dve.scalar_tensor_tensor(prob[:, b, 0, :], prob[:, b, 1, :], cmix[:, b:b + 1], prob[:, b, 0, :],
                                             ALU.mult, ALU.add).then_inc(comb_done, 1)

            def output(g, t):
                b, n = t % 2, g.step(t)
                dve.wait_ge(u_half, n + 1)
                if g.na:
                    for m in range(2):
                        cols = slice(m * HD, (m + 1) * HD)
                        last = dve.scalar_tensor_tensor(u[:, b, cols], mix[:, m * P + HD:(m + 1) * P],
                                                        rrec[:, b, m:m + 1], u_hi[:, cols], ALU.mult, ALU.add)
                    last.then_inc(u_done, 1)
                else:
                    dve.scalar_tensor_tensor(u[:, b, :], mix[:, P:2 * P], rrec[:, b, 0:1], u_hi[:], ALU.mult, ALU.add)\
                        .then_inc(u_done, 1)

            def gated(g, t):
                cols, src = slice(t * P, (t + 1) * P), turn_bank(g.na, ("U", t))[:, 0:P]
                dve.wait_ge(turned, g.use("U", t) + 1)
                dve.wait_ge(gate_silu, g.step(t) + 1)
                if t == 0:
                    reached(dve, mixed_out, 16 * g.stores())
                if g.na:
                    dve.tensor_tensor(mixed[:, cols], src, gate[:, cols], ALU.mult).then_inc(turn_freed, 1)
                else:
                    dve.scalar_tensor_tensor(mixed[:, cols], src, sgain[:, bass.ds(g.l, 1)], gate[:, cols],
                                             ALU.mult, ALU.mult).then_inc(turn_freed, 1)

            def inner_bias(g):
                n = g.l * NA_G + g.i
                dve.wait_ge(edge_masked, n + 1)
                dve.tensor_copy(inner[:], edge[:, :, 2 * W:11 * W]).then_inc(inner_copied, 1)
                dve.wait_ge(inner_copied, n + 1)
                dve.memset(inner[0:W, :, 8 * W:9 * W], MASKED).then_inc(inner_ready, 1)
                dve.memset(inner[W:P, :, 0:W], MASKED).then_inc(inner_ready, 1)
                dve.wait_ge(inner_ready, 2 * n + 2)

            def take_mixed(l, i):
                dve.wait_ge(h_hi_done, l * (2 * NT + 1) + NT + i + 1)
                dve.tensor_tensor(h_lo[:, i, :], f32(h_lo[:, i, :]), f32(h_hi[:, i, :]), ALU.subtract)\
                    .then_inc(h_ready, 1)

            def attend(g):
                if g.na:
                    inner_bias(g)
                for t in range(NT + 2):
                    for c in range(2):
                        if t < NT:
                            shifted(g, t, c)
                    for c in range(3 if g.na and 1 <= t <= NT and INNER[t - 1] else 2):
                        if t == 0:
                            v_part(g, c)
                        if 1 <= t <= NT:
                            p_part(g, t - 1, c)
                    if t < NT:
                        combine(g, t)
                    if g.projects(t):
                        piece_part(g, t)
                    if 1 <= t <= NT:
                        silu(g, t - 1)
                        output(g, t - 1)
                    if t >= 2:
                        gated(g, t - 2)
                    if not g.project:
                        for i in TAKEN.get(t, ()):
                            take_mixed(g.l, i)

            with dve.Fori(0, DEPTH) as l:
                norm_stats(l)
                first = First(l)

                def lo_of(i):
                    dve.wait_ge(h_hi_done, l * (2 * NT + 1) + i + 1)
                    dve.tensor_tensor(h_lo[:, i, :], normed[i % 4], f32(h_hi[:, i, :]), ALU.subtract)\
                        .then_inc(h_ready, 1)

                for i in range(NT):
                    if i >= 4:
                        norm_ready(dve, l, i - 4)
                    dve.scalar_tensor_tensor(normed[i % 4], xt[:, i, :], ngain[:, bass.ds(l * NT + i, 1)],
                                             scores[:, 0, :], ALU.mult, ALU.mult).then_inc(norm_done, 1)
                    if i % 2:
                        lo_of(i - 1)
                for t in First.STEPS:
                    piece_part(first, t)
                groups(dve, l, attend)
                for hf in range(2):
                    cols = slice(hf * HALF, (hf + 1) * HALF)
                    dve.wait_ge(h_hi_done, l * (2 * NT + 1) + 2 * NT + hf)
                    dve.tensor_tensor(h_lo[:, NT - 1, cols], mixed[:, cols], f32(h_hi[:, NT - 1, cols]),
                                      ALU.subtract).then_inc(h_ready, 1)
                for t in range(2 * NT):
                    n = l * 2 * CPL + GROUPS * NT + t
                    cols = slice((t % 2) * HALF, (t % 2 + 1) * HALF)
                    reached(dve, piece_done, n + 1)
                    dve.tensor_tensor(xt[:, t // 2, cols], xt[:, t // 2, cols], proj[:, t % 2], ALU.add)\
                        .then_inc(piece_freed, 1)
            norm_stats(DEPTH)
            for i in range(NT):
                if i >= 4:
                    dve.wait_ge(stored[i % 4], 16)
                dve.scalar_tensor_tensor(normed[i % 4], xt[:, i, :], fgain[:, i:i + 1], scores[:, 0, :],
                                         ALU.mult, ALU.mult).then_inc(norm_done, 1)


def kernel(x, norm_g, w_in, w_out, lam_q1, lam_k1, lam_q2, lam_k2, subln_g, rpb, final_g):
    import concourse.bacc as bacc
    from concourse.bass_utils import run_bass_kernel_spmd

    f = lambda a: np.asarray(a)
    x, norm_g, w_in, w_out, subln_g, rpb, final_g = map(f, (x, norm_g, w_in, w_out, subln_g, rpb, final_g))
    depth, D, _ = w_in.shape
    S = x.shape[1]
    cut = lambda w: w.reshape(depth, D // P, P, -1, P).transpose(0, 3, 2, 1, 4)
    by_out = cut(w_in)
    q, k, v = [list(range(4 * j, 4 * j + 4)) + list(range(12 + 4 * j, 16 + 4 * j)) for j in range(3)]
    order = [v[0], k[0], q[0]]
    for g in range(8):
        order += [24 + g] + ([v[g + 1], k[g + 1], q[g + 1]] if g < 7 else [])
    stream = np.concatenate([by_out[:, order], cut(w_out)], axis=1).reshape(-1, P, D)
    stream = np.concatenate([stream, stream[:1]])
    gap = np.zeros(64, rpb.dtype)
    columns = lambda a: np.ascontiguousarray(a.reshape(-1, P).T)
    arrays = {
        "x_t": x[0].T,
        "chunks": stream,
        "norm_gain": columns(norm_g),
        "final_gain": columns(final_g),
        "subln_gain": columns(subln_g),
        "lam_vecs": np.stack([f(lam_q1), f(lam_k1), f(lam_q2), f(lam_k2)])[None],
        "bias_rows": np.concatenate([gap, rpb.ravel(), gap]),
    }
    arrays = {n: np.ascontiguousarray(a) for n, a in arrays.items()}
    nc = bacc.Bacc("TRN2", target_bir_lowering=False, num_devices=1)
    aps = [nc.dram_tensor(n, a.shape, mybir.dt.from_np(a.dtype), kind="ExternalInput").ap() for n, a in arrays.items()]
    out = nc.dram_tensor("out_t", (D, S), F32, kind="ExternalOutput").ap()
    hybrid_encoder(nc, *aps, out)
    r = run_bass_kernel_spmd(nc, [arrays], core_ids=[0])
    return np.ascontiguousarray(r.results[0]["out_t"].T)[None]
```

```python
import numpy as np
import concourse.bass as bass
from concourse import mybir
from contextlib import ExitStack

ALU = mybir.AluOpType
ACT = mybir.ActivationFunctionType
F32 = mybir.dt.float32
F32R = mybir.dt.float32r
FP16 = mybir.dt.float16
I32 = mybir.dt.int32

P = 128
HALF = 512
MASKED = -1e30


def hybrid_encoder(nc, x_t, chunks, norm_gain, final_gain, subln_gain, lam_vecs, bias_rows, out_t):
    D, S = x_t.shape
    NT = D // P
    DEPTH = norm_gain.shape[1] // NT
    HD = lam_vecs.shape[3]
    DA_G, NA_G = 4, 4
    GROUPS = DA_G + NA_G
    RB = 2 * 16 - 1
    RR = 15
    W = 64
    CPL = 4 * GROUPS + NT + 1
    EPS = 1e-6
    EDGE = 14
    LAM_INIT = [0.8 - 0.6 * float(np.exp(-0.3 * l)) for l in range(DEPTH)]
    SLOPES = [2.0 ** (-8.0 * (i + 1) / DA_G) for i in range(DA_G)]
    OFF = S - P
    MADE = 9
    CONSTS = 2 + 2 * DEPTH
    G_, V_, K_, Q_ = range(4)
    LEAD = 6
    IN = 2 * 4 * GROUPS
    EARLY = NT
    LATE = [8, 9, 0, 1, 2, 3, 4, 5, 6, 7, 10, 11, 12, 13, 14, 15]
    PPL = IN + EARLY + len(LATE)
    LAST_ROWS = 5
    TILE_OF = [0, 1, 2, 3, 4, None, 5, 6, 7]
    USED_UP = [2, 4, 6, 8, 10, 18, 20, 22, 24]
    LAST_CHUNKS = {2: 1, 6: 2, 7: 3, 8: 4}
    TAKEN = {2: [0], 3: [1, 2, 3], 4: [4, 5], 5: [6]}
    both = lambda ks: [(t, [k]) for k in ks for t in (0, 1)]
    most = range(NT - 1)
    LATE_CHUNKS = {USED_UP[j - 2] - EARLY: j for j in range(LAST_ROWS, NT + 1)}
    LAST_FILL = {1: [], 2: [], 3: [[], [], both([0])], 4: [both([1]), both([2]), both([3])],
                 5: [[], both([4]), both([5])], 6: [both([6]), [(2, range(0, 3))], [(2, range(3, 7))]],
                 7: [[(3, range(0, 3))], [(3, range(3, 7)), (4, range(0, 2))], [(4, range(2, 7))]],
                 8: [[(5, range(0, 4))], [(5, range(4, 7))], [(6, most)], [(7, most)]]}

    TILE = {False: list(range(NT)), True: [0, 1, 6, 7, 2, 3, 4, 5]}
    KEY0 = [min(max(2 * tile - 4, 0), 8) for tile in TILE[True]]
    INNER = [2 <= tile <= 5 for tile in TILE[True]]
    WIDTH = [576 if INNER[t] else 512 for t in range(NT)]
    STEP0 = {na: min(t for t in range(NT) if TILE[na][t] >= NT // 2) for na in TILE}

    def uses(na):
        order, split = {}, {}
        def use(key, halves):
            order[key] = len(order)
            if halves:
                split[key] = len(split)
        use(("V", 0), True)
        use(("V", 1), True)
        use("before", False)
        for t in range(1, NT + 1):
            for c in range(3 if na and INNER[t - 1] else 2):
                use(("T", t - 1, c), True)
            if t >= 2:
                use(("U", t - 2), False)
        return order, split

    def half(t):
        return slice((t % 2) * HALF, (t % 2 + 1) * HALF)

    def same_half(order, q):
        return max((p for p in range(q) if order[p] % 2 == order[q] % 2), default=None)

    ORDER = {na: uses(na)[0] for na in (False, True)}
    SPLIT = {na: uses(na)[1] for na in (False, True)}
    ORDERS = DA_G * len(ORDER[False]) + NA_G * len(ORDER[True]) + 1
    SPLITS = DA_G * len(SPLIT[False]) + NA_G * len(SPLIT[True])

    def chunk_of(t):
        return TILE_OF.index(t // 2)

    def out_number(l, t):
        return l * PPL + IN + (t if t < EARLY else EARLY + LATE.index(t))

    class Group:

        def __init__(self, l, na, i, project=True):
            self.l, self.na, self.i, self.project = l, na, i, project
            self.g = i + (DA_G if na else 0)

        def step(self, t):
            return self.l * (GROUPS * NT) + self.g * NT + t

        def kind_step(self, t):
            return self.l * (DA_G * NT) + self.i * NT + t

        def group(self):
            return self.l * GROUPS + self.g

        def use(self, *key):
            first = DA_G * len(ORDER[False]) if self.na else 0
            if key == ("U", NT - 1):
                at = len(ORDER[self.na]) + (ORDER[self.na]["before"] if self.project else 0)
            else:
                at = ORDER[self.na][key]
            return self.l * ORDERS + first + self.i * len(ORDER[self.na]) + at

        def split(self, *key):
            first = DA_G * len(SPLIT[False]) if self.na else 0
            return self.l * SPLITS + first + self.i * len(SPLIT[self.na]) + SPLIT[self.na][key]

        def piece(self, t):
            return self.l * PPL + LEAD + self.g * NT + t

        def chunk(self, t):
            return self.l * CPL + LEAD // 2 + self.g * 4 + t // 2

        def projects(self, t):
            return t < NT and (self.project or t // 2 == G_)

        def taken(self, t):
            return self.l * (4 * GROUPS) + 2 + self.g * 4 + (2 if t // 2 == Q_ else 0) + t % 2

        def stores(self):
            return self.l * (GROUPS - 1) + self.g

    class First(Group):

        STEPS = range(NT - LEAD, NT)

        def __init__(self, l):
            self.l, self.na, self.i, self.g, self.project = l, False, -1, -1, True

    with ExitStack() as ctx:
        def sb(name, shape, dt=F32):
            return ctx.enter_context(nc.sbuf_tensor(name, shape, dt))

        def sem(name):
            return ctx.enter_context(nc.semaphore(name))

        xt = sb("xt", [P, NT, S])
        h_hi = sb("h_hi", [P, NT, S], F32R)
        h_lo = sb("h_lo", [P, NT, S], F32R)
        w_raw = sb("w_raw", [P, NT, P])
        w_hi = sb("w_hi", [P, 2, NT, P], F32R)
        w_lo = sb("w_lo", [P, 2, NT, P], F32R)
        q_two = sb("q_two", [P, 2, S], F32R)
        k_two = sb("k_two", [P, 2, S], F32R)
        k_lo = sb("k_lo", [P, S], F32R)
        k_next = sb("k_next", [P, S])
        v_next = sb("v_next", [P, S])
        v_hl = sb("v_hl", [P, NT, 256], F32R)
        gate = sb("gate", [P, S])
        gate_exp = sb("gate_exp", [P, S])
        prob = sb("prob", [P, 2, 2, S])
        pt_hi = sb("pt_hi", [P, 2, HALF], F32R)
        pt_lo = sb("pt_lo", [P, 2, HALF], F32R)
        px_hi = sb("px_hi", [HD, 256], F32R)
        px_lo = sb("px_lo", [HD, 256], F32R)
        dist = sb("dist", [P, OFF + S], FP16)
        edge = sb("edge", [P, 2, EDGE * W])
        inner = sb("inner", [P, 2, 9 * W])
        u_hi = sb("u_hi", [P, P])
        u = sb("u", [P, 2, P])
        ident = sb("ident", [P, P])
        ones = sb("ones", [P, 1])
        colmask = sb("colmask", [P, W])
        ngain = sb("ngain", [P, DEPTH * NT])
        fgain = sb("fgain", [P, NT])
        sgain = sb("sgain", [P, DEPTH])
        qscale = sb("qscale", [P, GROUPS])
        escale = sb("escale", [P, DA_G])
        escale_now = sb("escale_now", [P, 1])
        nescale = sb("nescale", [P, DA_G])
        neglam = sb("neglam", [P, DEPTH])
        mx = sb("mx", [P, 2, 2])
        nm = sb("nm", [P, 2, 2])
        rsum = sb("rsum", [P, 2, 2])
        rrec = sb("rrec", [P, 2, 2])
        cmix = sb("cmix", [P, 2])
        ssq = sb("ssq", [P, 2])
        msq = sb("msq", [P, 2])
        rms = sb("rms", [P, 2])
        power = sb("power", [P, NT])
        stat = sb("stat", [P, NT])
        rinv = sb("rinv", [P, NT])
        lam_s = sb("lam_s", [P, 2, DEPTH])
        lam_e = sb("lam_e", [P, 2, DEPTH])
        squares = prob[:, 0, 0, :]
        square = prob[:, 0, 1, :]
        lam_in = gate[:, 0:4 * DEPTH * HD].rearrange("p (a l d) -> p a l d", a=4, l=DEPTH)
        normed = [prob[:, 1, 0, :], prob[:, 1, 1, :], square, squares]

        scores = ctx.enter_context(nc.psum_tensor("scores", [P, 2, S], F32))
        proj = ctx.enter_context(nc.psum_tensor("proj", [P, 2, HALF], F32))
        turn = ctx.enter_context(nc.psum_tensor("turn", [P, HALF], F32))
        mix = ctx.enter_context(nc.psum_tensor("mix", [P, HALF], F32))
        all_scores = scores[:].rearrange("p m s -> p (m s)")

        def turn_bank(na, key):
            if not na and key == ("V", 1):
                return proj[:, 1]
            return all_scores[:, 3 * HALF:] if na and ORDER[na].get(key, 0) % 2 else turn[:]

        def window(t, m):
            return m * (3 * HALF - WIDTH[t])

        def bank(g, t):
            return scores[:, 1, (t % 2) * HALF:(t % 2 + 1) * HALF] if isinstance(g, First) and t // 2 == K_ else proj[:, t % 2]

        mixed_dram = nc.dram_tensor("mixed_dram", (D, S), F32).ap()
        bias_dram = nc.dram_tensor("bias_dram", (DEPTH * 2 * NA_G, W, RR * W), F32).ap()

        x_in = [sem(f"x_in{i}") for i in range(NT)]
        const_in = sem("const_in")
        lam_loaded = sem("lam_loaded")
        bias_spread = sem("bias_spread")
        w_in = sem("w_in")
        edge_in = sem("edge_in")
        mixed_out = [sem(f"mixed_out{hf}") for hf in range(2)]
        mixed_in = [sem(f"mixed_in{i}") for i in range(NT)]
        stored = [sem(f"stored{b}") for b in range(len(normed))]
        made = sem("made")
        lam_dot = sem("lam_dot")
        lam_exp = sem("lam_exp")
        consts_done = sem("consts_done")
        dist_int = sem("dist_int")
        w_hi_done = sem("w_hi_done")
        w_lo_done = sem("w_lo_done")
        sq_done = sem("sq_done")
        sum_done = sem("sum_done")
        stat_mm = sem("stat_mm")
        stat_done = sem("stat_done")
        rinv_done = sem("rinv_done")
        spread_mm = sem("spread_mm")
        norm_done = sem("norm_done")
        h_hi_done = sem("h_hi_done")
        h_ready = sem("h_ready")
        h_ready_pool = sem("h_ready_pool")
        piece_done = sem("piece_done")
        piece_half = sem("piece_half")
        piece_freed = sem("piece_freed")
        gate_plus = sem("gate_plus")
        gate_rec = sem("gate_rec")
        gate_silu = sem("gate_silu")
        q_ready = sem("q_ready")
        k_hi_done = sem("k_hi_done")
        k_ready = sem("k_ready")
        k_lo_done = sem("k_lo_done")
        edge_masked = sem("edge_masked")
        inner_copied = sem("inner_copied")
        inner_ready = sem("inner_ready")
        tail_done = sem("tail_done")
        qk_done = sem("qk_done")
        scores_read = sem("scores_read")
        shift_ready = sem("shift_ready")
        exp_done = sem("exp_done")
        escale_set = sem("escale_set")
        rrec_done = sem("rrec_done")
        cmix_done = sem("cmix_done")
        comb_done = sem("comb_done")
        turned = sem("turned")
        turn_hi = sem("turn_hi")
        turn_freed = sem("turn_freed")
        pv_done = sem("pv_done")
        u_half = sem("u_half")
        u_done = sem("u_done")
        ssq_done = sem("ssq_done")
        msq_done = sem("msq_done")
        rms_done = sem("rms_done")
        un_done = sem("un_done")

        f32 = lambda t: t.bitcast(F32)
        HR = NT // 2 + NT + 1

        def norm_ready(e, l, k):
            if k % 2:
                e.wait_ge(h_ready_pool, l * (NT // 2) + k // 2 + 1)
            else:
                e.wait_ge(h_ready, l * HR + k // 2 + 1)

        def groups(e, l, attend):
            with e.Fori(0, DA_G - 1) as i:
                attend(Group(l, False, i), Group(l, False, i + 1))
            attend(Group(l, False, DA_G - 1), Group(l, True, 0))
            with e.Fori(0, NA_G - 1) as i:
                attend(Group(l, True, i), Group(l, True, i + 1))
            attend(Group(l, True, NA_G - 1, project=False), None)

        def steps(g, behind):
            for t in range(1, NT):
                yield t, g, t
            yield NT, behind, 0

        begun = {e: sem(f"begun_{e}") for e in ("act", "dve", "pe", "pool")}

        def reached(e, count, n):
            e.wait_ge(count, n + 1)

        def start_at_one(e, *counts):
            for count in counts:
                e.sem_inc(count, 1)

        def begin(e, name):
            e.sem_inc(begun[name], 1)

        block = ctx.enter_context(nc.Block())

        @block.sync
        def _(sp):
            start_at_one(sp, *mixed_out)
            for i in range(NT):
                sp.dma_start(xt[:, i, :], x_t[i * P:(i + 1) * P, :]).then_inc(x_in[i], 16)
                if i == 0:
                    sp.dma_start(w_raw[:], chunks[0].rearrange("p (t c) -> p t c", c=P)).then_inc(w_in, 16)
            sp.dma_start(ngain[:], norm_gain).then_inc(const_in, 16)
            sp.dma_start(fgain[:], final_gain).then_inc(const_in, 16)
            sp.dma_start(sgain[:], subln_gain).then_inc(const_in, 16)
            sp.dma_start(lam_in, bass.AP(lam_vecs.tensor, 0, [[0, P], [1, 4 * DEPTH * HD]])
                         .rearrange("p (a l d) -> p a l d", a=4, l=DEPTH)).then_inc(lam_loaded, 16)
            sp.wait_ge(w_lo_done, 1)
            sp.dma_start(w_raw[:], chunks[1].rearrange("p (t c) -> p t c", c=P)).then_inc(w_in, 16)
            for h in range(DEPTH * 2 * NA_G):
                sp.dma_start(bias_dram[h].rearrange("q (r k) -> r q k", k=W),
                             bass.AP(bias_rows.tensor, W + h * RR * RB + 15, [[RB, RR], [-1, W], [1, W]]))\
                    .then_inc(bias_spread, 16)

            def load_chunk(c):
                sp.wait_ge(w_lo_done, c)
                sp.dma_start(w_raw[:], chunks[bass.ds(c, 1)].rearrange("o p (t c) -> (o p) t c", c=P))\
                    .then_inc(w_in, 16)

            def load_edge(l, i):
                sp.wait_ge(bias_spread, 16 * DEPTH * 2 * NA_G)
                for hd in range(2):
                    for odd in range(2):
                        sp.dma_start(edge[odd * W:(odd + 1) * W, hd, :],
                                     bias_dram[bass.ds(l * 2 * NA_G + 2 * i + hd, 1), :,
                                               (1 - odd) * W:(1 - odd + EDGE) * W].rearrange("o q k -> (o q) k"))\
                            .then_inc(edge_in, 16)

            def store_half(g, hf, t):
                reached(sp, turn_freed, g.use("U", t) + 1)
                sp.dma_start(mixed_dram[bass.ds(g.g * P, P), half(hf)], gate[:, half(hf)]).then_inc(mixed_out[hf], 16)

            def attend(g, behind):
                for t, front, ft in steps(g, behind):
                    if front and front.projects(ft) and ft % 2 == 0:
                        load_chunk(front.chunk(ft) + 1)
                    if t == 4 and behind and behind.na:
                        reached(sp, scores_read, 2 * g.step(4))
                        load_edge(g.l, behind.i)
                if behind:
                    store_half(g, 0, STEP0[True] + 3 if g.na else STEP0[False] - 1)
                    store_half(g, 1, NT - 1)
                else:
                    load_chunk(g.l * CPL + 4 * GROUPS + 1)
                    reached(sp, piece_done, g.l * PPL + IN)
                    for hf in range(2):
                        reached(sp, mixed_out[hf], 16 * g.stores())
                    for i in range(NT - 1):
                        sp.dma_start(f32(h_lo[:, i, :]), mixed_dram[i * P:(i + 1) * P, :])\
                            .then_inc(mixed_in[i], 16)

            with sp.Fori(0, DEPTH) as l:
                for c in range(2, LEAD // 2 + 2):
                    load_chunk(l * CPL + c)
                groups(sp, l, attend)
                for j in range(2, NT + 1):
                    load_chunk(l * CPL + 4 * GROUPS + j)
                for c in range(2):
                    load_chunk((l + 1) * CPL + c)
            for i in range(NT):
                sp.wait_ge(norm_done, DEPTH * NT + i + 1)
                sp.dma_start(out_t[i * P:(i + 1) * P, :], normed[i % 4]).then_inc(stored[i % 4], 16)
            for b in range(4):
                sp.wait_ge(stored[b], 16 * NT // 4)
            sp.wait_ge(w_in, 16 * (DEPTH * CPL + 2))
            sp.wait_ge(const_in, 48)

        @block.gpsimd
        def _(pool):
            pool.memset(ident[:], 0.0).then_inc(made, 1)
            pool.memset(colmask[:], 0.0).then_inc(made, 1)
            pool.memset(ones[:], 1.0).then_inc(made, 1)
            pool.memset(power[:], -0.5).then_inc(made, 1)
            for i in range(DA_G):
                pool.memset(qscale[:, i:i + 1], HD ** -0.5 / SLOPES[i])
                pool.memset(escale[:, i:i + 1], SLOPES[i])
                pool.memset(nescale[:, i:i + 1], -SLOPES[i])
            pool.memset(qscale[:, DA_G:], HD ** -0.5)
            table = prob[:, 1].bitcast(I32).rearrange("p m s -> p (m s)")[:, 0:OFF + S]
            pool.iota(table, pattern=[[1, OFF + S]], base=-OFF, channel_multiplier=-1).then_inc(dist_int, 1)
            pool.wait_ge(made, 4)
            pool.affine_select(out=ident[:], in_=ident[:], compare_op=ALU.not_equal, fill=1.0, base=0,
                               pattern=[[-1, P]], channel_multiplier=1).then_inc(made, 1)
            n = 5
            for first, base, sign in ((0, 8, 1), (16, 7 - 16, -1)):
                for r in range(2):
                    part = colmask[r * W:(r + 1) * W, first:first + 48]
                    pool.wait_ge(made, n)
                    pool.affine_select(out=part, in_=part, compare_op=ALU.is_ge, fill=MASKED, base=base,
                                       pattern=[[sign, 48]], channel_multiplier=-sign).then_inc(made, 1)
                    n += 1
            pool.wait_ge(made, MADE)

            def w_lo_part(c, b):
                pool.wait_ge(w_hi_done, c + 1)
                pool.tensor_tensor(w_lo[:, b], w_raw[:], f32(w_hi[:, b]), ALU.subtract).then_inc(w_lo_done, 1)

            def out_lo_part(l, j):
                w_lo_part(l * CPL + 4 * GROUPS + j, j % 2)

            def mask_edge(l, i):
                pool.wait_ge(edge_in, 64 * (l * NA_G + i + 1))
                pool.wait_ge(made, MADE)
                rows = edge[:].rearrange("p h (r k) -> p (h r) k", k=W)
                pool.tensor_tensor(rows, rows, colmask[:].unsqueeze(1).to_broadcast([P, 2 * EDGE, W]), ALU.add)\
                    .then_inc(edge_masked, 1)

            def silu(g, t):
                cols = slice(t * P, (t + 1) * P)
                pool.wait_ge(gate_rec, g.step(t) + 1)
                pool.tensor_tensor(gate[:, cols], gate[:, cols], gate_exp[:, cols], ALU.mult).then_inc(gate_silu, 1)

            def normalise(g, t):
                b, n = t % 2, g.kind_step(t)
                pool.wait_ge(ssq_done, n + 1)
                begin(pool, "pool")
                pool.tensor_scalar(msq[:, b:b + 1], ssq[:, b:b + 1], 1.0 / P, EPS, ALU.mult, ALU.add)\
                    .then_inc(msq_done, 1)
                pool.wait_ge(msq_done, n + 1)
                pool.tensor_tensor(rms[:, b:b + 1], msq[:, b:b + 1], power[:, 0:1], ALU.pow).then_inc(rms_done, 1)
                pool.wait_ge(rms_done, n + 1)
                begin(pool, "pool")
                pool.tensor_scalar(u[:, b, :], u[:, b, :], rms[:, b:b + 1], None, ALU.mult).then_inc(un_done, 1)

            def attend(g, behind):
                for t, front, ft in steps(g, behind):
                    if front and front.projects(ft) and ft % 2 == 0:
                        w_lo_part(front.chunk(ft) + 1, (ft // 2) % 2)
                    if not g.na:
                        silu(g, t - 1)
                        normalise(g, t - 1)
                    if t == 5 and behind and behind.na:
                        mask_edge(g.l, behind.i)
                    if not behind and t in LAST_CHUNKS:
                        out_lo_part(g.l, LAST_CHUNKS[t])

            def norm_stats(n):
                pool.wait_ge(stat_done, n + 1)
                pool.tensor_tensor(rinv[:], stat[:], power[:], ALU.pow).then_inc(rinv_done, 1)

            def add_square(n, order, q):
                cols = half(order[q])
                pool.wait_ge(sq_done, n + q + 1)
                if same_half(order, q) is None:
                    pool.nop().then_inc(sum_done, 1)
                else:
                    pool.tensor_tensor(squares[:, cols], squares[:, cols], square[:, cols], ALU.add)\
                        .then_inc(sum_done, 1)

            for b in range(2):
                w_lo_part(b, b)
            norm_stats(0)
            with pool.Fori(0, DEPTH) as l:
                first = First(l)
                for i in range(1, NT, 2):
                    pool.wait_ge(h_hi_done, l * (2 * NT + 1) + i + 1)
                    pool.tensor_tensor(h_lo[:, i, :], normed[i % 4], f32(h_hi[:, i, :]), ALU.subtract)\
                        .then_inc(h_ready_pool, 1)
                for t in First.STEPS[2::2]:
                    w_lo_part(first.chunk(t) + 1, (t // 2) % 2)
                w_lo_part(Group(l, False, 0).chunk(0) + 1, 0)
                groups(pool, l, attend)
                for q in range(len(LATE)):
                    if q in LATE_CHUNKS:
                        out_lo_part(l, LATE_CHUNKS[q])
                    add_square((l + 1) * 2 * NT, LATE, q)
                norm_stats(l + 1)
                for b in range(2):
                    w_lo_part((l + 1) * CPL + b, b)

        @block.scalar
        def _(act):
            start_at_one(act, exp_done)

            def square_of(n, order, q):
                t, before = order[q], same_half(order, q)
                dst = squares if before is None else square
                if before is not None:
                    act.wait_ge(sum_done, n + before + 1)
                act.activation(dst[:, half(t)], xt[:, t // 2, half(t)], ACT.Square).then_inc(sq_done, 1)

            for q in range(2 * NT):
                if q % 2 == 0:
                    act.wait_ge(x_in[q // 2], 16)
                if q == 2:
                    act.wait_ge(w_in, 16)
                    act.activation(w_hi[:, 0], w_raw[:], ACT.Copy).then_inc(w_hi_done, 1)
                square_of(0, range(2 * NT), q)
            act.wait_ge(w_in, 32)
            act.activation(w_hi[:, 1], w_raw[:], ACT.Copy).then_inc(w_hi_done, 1)
            act.wait_ge(lam_dot, 2 * DEPTH)
            act.activation(lam_e[:], lam_s[:], ACT.Exp).then_inc(lam_exp, 1)

            def w_hi_part(c, b, freed):
                act.wait_ge(w_in, 16 * (c + 1))
                reached(act, piece_done, freed)
                act.activation(w_hi[:, b], w_raw[:], ACT.Copy).then_inc(w_hi_done, 1)

            def piece_part(g, t):
                ps, n, kind = bank(g, t), g.piece(t), t // 2
                cols = slice((t % 2) * HALF, (t % 2 + 1) * HALF)
                if kind == G_:
                    reached(act, piece_done, n + 1)
                    act.activation(gate_exp[:, cols], ps, ACT.Exp, scale=-1.0).then_inc(piece_half, 1)
                if kind == Q_:
                    reached(act, piece_done, n + 1)
                    if not isinstance(g, First):
                        act.wait_ge(qk_done, g.step(t if t % 2 == 0 else NT))
                    col = qscale[:, bass.ds(g.g + 1, 1)]
                    begin(act, "act")
                    for m in range(2):
                        own = slice(m * HD, (m + 1) * HD)
                        last = act.activation(q_two[own, m, cols], ps[own], ACT.Copy, scale=col[own])
                    last.then_inc(piece_half, 1)

            def k_hi_part(g):
                if not isinstance(g, First):
                    act.wait_ge(qk_done, g.step(NT))
                act.wait_ge(piece_freed, g.piece(2 * K_ + 1) + 1)
                for m in range(2):
                    own = slice(m * HD, (m + 1) * HD)
                    act.activation(k_two[own, m], k_next[own], ACT.Copy).then_inc(k_hi_done, 1)

            def k_again_part(g):
                for m in range(2):
                    own, other = slice(m * HD, (m + 1) * HD), slice((1 - m) * HD, (2 - m) * HD)
                    act.activation(k_two[other, m], k_next[own], ACT.Copy).then_inc(k_ready, 1)

            def turn_part(g, key, dst, src):
                act.wait_ge(turned, g.use(*key) + 1)
                act.activation(dst, src, ACT.Copy).then_inc(turn_hi, 1)

            def v_part(g, c):
                src = turn_bank(g.na, ("V", c))
                if g.na:
                    dst = v_hl[:, 4 * c:4 * c + 4].rearrange("p k (h s e) -> p k h s e", h=2, s=2)[:, :, :, 0, :]
                    src = src.rearrange("p (k h e) -> p k h e", k=4, h=2)
                else:
                    dst, src = v_hl[:, 4 * c:4 * c + 4, 0:P], src.rearrange("p (k e) -> p k e", k=4)
                turn_part(g, ("V", c), dst, src)

            def p_part(g, t, c):
                reached(act, pv_done, g.step(t))
                src = turn_bank(g.na, ("T", t, c))
                if c == 2:
                    turn_part(g, ("T", t, c), px_hi[:], src[0:HD, 0:256])
                else:
                    turn_part(g, ("T", t, c), pt_hi[:, c, :], src)

            def exponentials(g, t, m):
                b = t % 2
                act.wait_ge(shift_ready, 2 * g.step(t) + m + 1)
                s = prob[:, b, m, 0:WIDTH[t] if g.na else S]
                scale = 1.0 if g.na else escale_now[:]
                act.activation(s, s, ACT.Exp, bias=nm[:, b, m:m + 1], scale=scale,
                               accum_out=rsum[:, b, m:m + 1]).then_inc(exp_done, 1)

            def output_half(g, t):
                b, n = t % 2, g.step(t)
                reached(act, pv_done, n + 1)
                act.wait_ge(rrec_done, n + 1)
                reached(act, u_done, n)
                if g.na:
                    for m in range(2):
                        last = act.activation(u_hi[:, m * HD:(m + 1) * HD], mix[:, m * P:m * P + HD], ACT.Copy,
                                              scale=rrec[:, b, m:m + 1])
                    last.then_inc(u_half, 1)
                else:
                    act.activation(u_hi[:], mix[:, 0:P], ACT.Copy, scale=rrec[:, b, 0:1]).then_inc(u_half, 1)
                    reached(act, u_done, n + 1)
                    act.activation(u_hi[:], u[:, b, :], ACT.Square, accum_out=ssq[:, b:b + 1]).then_inc(ssq_done, 1)

            def take_mixed(l, i):
                act.wait_ge(mixed_in[i], 16 * (l + 1))
                act.activation(h_hi[:, i, :], f32(h_lo[:, i, :]), ACT.Copy).then_inc(h_hi_done, 1)

            def begin_group(g):
                if not g.na:
                    reached(act, exp_done, 2 * g.step(0))
                    act.activation(escale_now[:], escale[:, bass.ds(g.i, 1)], ACT.Copy).then_inc(escale_set, 1)
                    act.wait_ge(escale_set, g.l * DA_G + g.i + 1)

            def attend(g, behind):
                for t, front, ft in steps(g, behind):
                    if front and front.projects(ft) and ft % 2 == 0:
                        w_hi_part(front.chunk(ft) + 1, (ft // 2) % 2, front.piece(ft))
                    if g.project and t == NT - 1:
                        k_hi_part(g)
                    if front and ft == 0:
                        begin_group(front)
                    for c in range(2):
                        p_part(g, t - 1, c)
                        if front:
                            exponentials(front, ft, c)
                    if g.na and INNER[t - 1]:
                        p_part(g, t - 1, 2)
                    if g.project and t == NT - 1:
                        k_again_part(g)
                    if front and front.projects(ft) and ft:
                        piece_part(front, ft)
                    output_half(g, t - 1)
                    if t == NT and behind:
                        for c in range(2):
                            v_part(behind, c)
                        piece_part(behind, 0)
                    if not behind:
                        if t in LAST_CHUNKS:
                            out_hi_part(g.l, LAST_CHUNKS[t])
                        for i in TAKEN.get(t, ()):
                            take_mixed(g.l, i)

            def out_hi_part(l, j):
                w_hi_part(l * CPL + 4 * GROUPS + j, j % 2, l * PPL + IN + (USED_UP[j - 2] if j > 1 else 0))

            with act.Fori(0, DEPTH) as l:
                first = First(l)
                for i in range(NT):
                    act.wait_ge(norm_done, l * NT + i + 1)
                    act.activation(h_hi[:, i, :], normed[i % 4], ACT.Copy).then_inc(h_hi_done, 1)
                for t in First.STEPS:
                    if t % 2 == 0 and t > 2:
                        w_hi_part(first.chunk(t) + 1, (t // 2) % 2, first.piece(t))
                    if t == 2 * Q_:
                        k_hi_part(first)
                        k_again_part(first)
                    piece_part(first, t)
                g = Group(l, False, 0)
                w_hi_part(g.chunk(0) + 1, 0, g.piece(0))
                begin_group(g)
                for c in range(2):
                    v_part(g, c)
                    exponentials(g, 0, c)
                piece_part(g, 0)
                groups(act, l, attend)
                last_group = Group(l, True, NA_G - 1, project=False)
                for hf, t in ((0, STEP0[True] + 3), (1, NT - 1)):
                    reached(act, turn_freed, last_group.use("U", t) + 1)
                    act.activation(h_hi[:, NT - 1, half(hf)], gate[:, half(hf)], ACT.Copy).then_inc(h_hi_done, 1)
                for q in range(len(LATE)):
                    if q in LATE_CHUNKS:
                        out_hi_part(l, LATE_CHUNKS[q])
                    act.wait_ge(piece_freed, l * PPL + IN + EARLY + q + 1)
                    square_of((l + 1) * 2 * NT, LATE, q)
                for b in range(2):
                    w_hi_part((l + 1) * CPL + b, b, (l + 1) * PPL)

        @block.tensor
        def _(pe):
            start_at_one(pe, pv_done, piece_done)

            def three(dst, a_hi, a_lo, b_hi, b_lo, start=True, stop=True):
                pe.matmul(dst, a_hi, b_hi, start=start, stop=False)
                pe.matmul(dst, a_hi, b_lo, start=False, stop=False)
                return pe.matmul(dst, a_lo, b_hi, start=False, stop=stop)

            def piece(dst, n, chunk, b, t, ks, ready=None):
                cols = slice((t % 2) * HALF, (t % 2 + 1) * HALF)
                if 0 in ks:
                    if n is not None:
                        pe.wait_ge(piece_freed, n - 1)
                    pe.wait_ge(w_lo_done, chunk + 1)
                for k in ks:
                    if ready:
                        ready(k)
                    last = three(dst, w_hi[:, b, k], w_lo[:, b, k], h_hi[:, k, cols], h_lo[:, k, cols],
                                 start=k == 0, stop=k == NT - 1)
                if NT - 1 in ks:
                    last.then_inc(piece_done, 1)

            def group_piece(g, t, ks):
                piece(bank(g, t), g.piece(t), g.chunk(t), (t // 2 + 1) % 2, t, ks)

            def score(g, t):
                reached(pe, scores_read, 2 * g.step(t))
                if t == 0:
                    pe.wait_ge(k_ready, 2 * g.group() + 2)
                    pe.wait_ge(k_lo_done, 2 * g.group() + 2)
                    pe.wait_ge(q_ready, 4 * g.group() + 2)
                if t == STEP0[g.na]:
                    pe.wait_ge(q_ready, 4 * g.group() + 4)
                tile = slice(TILE[g.na][t] * P, (TILE[g.na][t] + 1) * P)
                first = KEY0[t] * W if g.na else 0

                def product(m, p, at, a, b):
                    out, cols = all_scores[:, at + a:at + b], slice(first + a, first + b)
                    if p == 0:
                        return pe.matmul(out, q_two[:, m, tile], k_two[:, m, cols], start=True, stop=False)
                    own = slice(m * HD, (m + 1) * HD)
                    return pe.matmul(out, q_two[own, m, tile], k_lo[own, cols], start=False, stop=True)

                at = [window(t, m) if g.na else m * S for m in range(2)]
                spans = [[(0, HALF)], [(WIDTH[t] - HALF, WIDTH[t])]] if g.na else [[(0, HALF), (HALF, S)]] * 2

                def tail(m, a, b):
                    for p in range(2):
                        last = product(m, p, at[m], a, b)
                    return last

                wide = g.na and INNER[t]
                if wide:
                    tail(0, HALF, WIDTH[t]).then_inc(tail_done, 1)
                for pair in zip(*spans):
                    for p in range(2):
                        for m in range(2):
                            last = product(m, p, at[m], *pair[m])
                if wide:
                    pe.wait_ge(tail_done, (g.l * NA_G + g.i) * sum(INNER) + sum(INNER[:t]) + 1)
                    last = tail(1, 0, WIDTH[t] - HALF)
                last.then_inc(qk_done, 1)

            def turn_wait(g, *key):
                if not g.na and key == ("V", 1):
                    pe.wait_ge(piece_freed, g.piece(0))
                else:
                    two_banks = g.na and key not in (("V", 0), ("U", NT - 1))
                    reached(pe, turn_freed, g.use(*key) - two_banks)
                return turn_bank(g.na, key)

            def turn_v(g, c):
                dst = turn_wait(g, "V", c)
                pe.wait_ge(piece_freed, g.piece(2 * V_) - NT + 2)
                for k in range(4):
                    last = pe.transpose(dst[:, k * P:(k + 1) * P], v_next[:, (4 * c + k) * P:(4 * c + k + 1) * P],
                                        ident[:])
                last.then_inc(turned, 1)

            def turn_p(g, t, c):
                dst = turn_wait(g, "T", t, c)
                if g.na:
                    reached(pe, exp_done, 2 * g.step(t) + min(c, 1) + 1)
                else:
                    pe.wait_ge(comb_done, g.kind_step(t) + 1)
                if c == 2:
                    begin(pe, "pe")
                    for m in range(2):
                        last = pe.transpose(dst[0:HD, m * P:(m + 1) * P], prob[:, t % 2, m, HALF:HALF + HD], ident[:])
                else:
                    m, first = (c, 0) if g.na else (0, c * HALF)
                    for k in range(4):
                        last = pe.transpose(dst[:, k * P:(k + 1) * P],
                                            prob[:, t % 2, m, first + k * P:first + (k + 1) * P], ident[:])
                last.then_inc(turned, 1)

            def weigh(g, t):
                last_turn = ("T", t, 2 if g.na and INNER[t] else 1)
                reached(pe, turn_freed, g.use(*last_turn) + 1)
                reached(pe, u_done, g.step(t))
                if not g.na:
                    for k in range(NT):
                        at = slice((k % 4) * P, (k % 4 + 1) * P)
                        pe.matmul(mix[:, 0:2 * P], pt_hi[:, k // 4, at], v_hl[:, k, :], start=k == 0, stop=False)
                        last = pe.matmul(mix[:, 0:P], pt_lo[:, k // 4, at], v_hl[:, k, 0:P], start=False,
                                         stop=k == NT - 1)
                else:
                    for m in range(2):
                        k0, o = KEY0[t] // 2, m * P
                        for k in range(4):
                            at = slice(k * P, (k + 1) * P)
                            pe.matmul(mix[:, o:o + P], pt_hi[:, m, at], v_hl[:, k0 + k, o:o + P], start=k == 0,
                                      stop=False)
                            last = pe.matmul(mix[:, o:o + HD], pt_lo[:, m, at], v_hl[:, k0 + k, o:o + HD],
                                             start=False, stop=k == 3 and not INNER[t])
                        if INNER[t]:
                            pe.matmul(mix[:, o:o + P], px_hi[:, o:o + P], v_hl[0:HD, k0 + 4, o:o + P],
                                      start=False, stop=False)
                            last = pe.matmul(mix[:, o:o + HD], px_lo[:, o:o + P], v_hl[0:HD, k0 + 4, o:o + HD],
                                             start=False, stop=True)
                last.then_inc(pv_done, 1)

            def turn_u(g, t):
                dst = turn_wait(g, "U", t)
                if g.na:
                    reached(pe, u_done, g.step(t) + 1)
                else:
                    pe.wait_ge(un_done, g.kind_step(t) + 1)
                pe.transpose(dst[:, 0:P], u[:, t % 2, :], ident[:]).then_inc(turned, 1)

            def out_piece(l, t, ks):
                n, end = out_number(l, t), NT - 1 if t < EARLY else NT
                if 0 in ks:
                    pe.wait_ge(piece_freed, n - 1)
                    pe.wait_ge(w_lo_done, l * CPL + 4 * GROUPS + chunk_of(t) + 1)
                for k in ks:
                    if t < 2:
                        pe.wait_ge(h_ready, l * HR + NT // 2 + k + 1)
                    if k == NT - 1:
                        pe.wait_ge(h_ready, l * HR + NT // 2 + k + t % 2 + 1)
                    b = chunk_of(t) % 2
                    last = three(proj[:, out_number(0, t) % 2], w_hi[:, b, k], w_lo[:, b, k], h_hi[:, k, half(t)],
                                 h_lo[:, k, half(t)], start=k == 0, stop=k == end - 1)
                if end - 1 in ks:
                    last.then_inc(piece_done, 1)

            def attend(g, behind):
                for t, front, ft in steps(g, behind):
                    last_step = t == NT and behind
                    if front and ft != 1:
                        score(front, ft)
                    parts = [range(0, 2), range(2, 5), range(5, 8)]
                    if last_step:
                        parts = [range(0, 2), range(2, 5), range(5, 8), ()]

                    def fill(j):
                        if not behind and LAST_FILL[t] and j < len(LAST_FILL[t]):
                            for p, ks in LAST_FILL[t][j]:
                                out_piece(g.l, p, ks)
                        if front and front.projects(ft):
                            group_piece(front, ft, parts[j])

                    fill(0)
                    turn_p(g, t - 1, 0)
                    fill(1)
                    turn_p(g, t - 1, 1)
                    if g.na and INNER[t - 1]:
                        turn_p(g, t - 1, 2)
                    fill(2)
                    if t >= 2:
                        turn_u(g, t - 2)
                    weigh(g, t - 1)
                    if last_step:
                        turn_v(behind, 0)
                        turn_v(behind, 1)
                        fill(3)
                        score(behind, 1)
                    elif t == NT:
                        fill(3)
                    if t == NT:
                        turn_u(g, NT - 1)

            def norm(n):
                pe.wait_ge(made, MADE)
                pe.wait_ge(sum_done, (n + 1) * 2 * NT)
                for i in range(NT):
                    last = pe.matmul(mix[:, i:i + 1], squares[:, i * P:(i + 1) * P], ones[:], start=True, stop=True)
                last.then_inc(stat_mm, 1)
                pe.wait_ge(rinv_done, n + 1)
                for i in range(NT):
                    last = pe.matmul(scores[:, 0, i * P:(i + 1) * P], rinv[:, i:i + 1].to_broadcast([P, P]), ident[:],
                                     start=True, stop=True)
                last.then_inc(spread_mm, 1)

            with pe.Fori(0, DEPTH) as l:
                norm(l)
                first = First(l)
                for j in range(2):
                    pe.wait_ge(w_lo_done, l * CPL + j + 1)
                for k in range(NT):
                    norm_ready(pe, l, k)
                    for t in First.STEPS[:4]:
                        b, cols = (t // 2 + 1) % 2, slice((t % 2) * HALF, (t % 2 + 1) * HALF)
                        last = three(bank(first, t), w_hi[:, b, k], w_lo[:, b, k], h_hi[:, k, cols],
                                     h_lo[:, k, cols], start=k == 0, stop=k == NT - 1)
                        if k == NT - 1:
                            last.then_inc(piece_done, 1)
                for t in First.STEPS[4:]:
                    group_piece(first, t, range(NT))
                g = Group(l, False, 0)
                score(g, 0)
                group_piece(g, 0, range(0, 4))
                turn_v(g, 0)
                group_piece(g, 0, range(4, 8))
                turn_v(g, 1)
                score(g, 1)
                reached(pe, turn_freed, g.use("V", 1) + 1)
                pe.sem_inc(turned, 1)
                groups(pe, l, attend)
                for q, t in enumerate(LATE):
                    if t >= EARLY:
                        out_piece(l, t, range(NT))
                    else:
                        pe.wait_ge(w_lo_done, l * CPL + 4 * GROUPS + LAST_ROWS + 1)
                        pe.wait_ge(piece_freed, l * PPL + IN + EARLY + q - 1)
                        pe.wait_ge(h_ready, l * HR + NT // 2 + NT + t % 2)
                        b = LAST_ROWS % 2
                        three(proj[:, q % 2], w_hi[:, b, t // 2], w_lo[:, b, t // 2], h_hi[:, NT - 1, half(t)],
                              h_lo[:, NT - 1, half(t)]).then_inc(piece_done, 1)
            norm(DEPTH)

        @block.vector
        def _(dve):
            start_at_one(dve, scores_read, turn_freed, u_done)
            dve.wait_ge(dist_int, 1)
            table = prob[:, 1].bitcast(I32).rearrange("p m s -> p (m s)")[:, 0:OFF + S]
            dve.scalar_tensor_tensor(dist[:], table, -1.0, table, ALU.mult, ALU.min).then_inc(consts_done, 1)
            for q in range(2 * NT):
                dve.wait_ge(sq_done, q + 1)
                cols = half(q)
                if q < 2:
                    dve.nop().then_inc(sum_done, 1)
                else:
                    dve.tensor_tensor(squares[:, cols], squares[:, cols], square[:, cols], ALU.add)\
                        .then_inc(sum_done, 1)
            dve.wait_ge(lam_loaded, 16)
            for l in range(DEPTH):
                for a in range(2):
                    dve.tensor_tensor_reduce(u[:, 0, 0:HD], lam_in[:, 2 * a, l], lam_in[:, 2 * a + 1, l], 1.0, 0.0,
                                             ALU.mult, ALU.add, lam_s[:, a, l:l + 1]).then_inc(lam_dot, 1)
                    dve.wait_ge(lam_dot, 2 * l + a + 1)
            dve.wait_ge(lam_exp, 1)
            dve.tensor_tensor(neglam[:], lam_e[:, 1], lam_e[:, 0], ALU.subtract).then_inc(consts_done, 1)
            dve.wait_ge(const_in, 48)
            dve.wait_ge(consts_done, 2)
            for l in range(DEPTH):
                dve.tensor_scalar(neglam[:, l:l + 1], neglam[:, l:l + 1], -LAM_INIT[l], None, ALU.add)\
                    .then_inc(consts_done, 1)
                dve.tensor_scalar(sgain[:, l:l + 1], sgain[:, l:l + 1], 1.0 - LAM_INIT[l], None, ALU.mult)\
                    .then_inc(consts_done, 1)
            dve.wait_ge(consts_done, CONSTS)

            def norm_stats(n):
                dve.wait_ge(stat_mm, n + 1)
                dve.tensor_scalar(stat[:], mix[:, 0:NT], 1.0 / D, EPS, ALU.mult, ALU.add).then_inc(stat_done, 1)
                dve.wait_ge(spread_mm, n + 1)

            def piece_part(g, t):
                ps, n, kind = bank(g, t), g.piece(t), t // 2
                cols = slice((t % 2) * HALF, (t % 2 + 1) * HALF)
                if kind == V_:
                    reached(dve, piece_done, n + 1)
                    dve.tensor_copy(v_next[:, cols], ps).then_inc(piece_freed, 1)
                if kind == K_:
                    reached(dve, piece_done, n + 1)
                    if not isinstance(g, First):
                        dve.wait_ge(k_ready, 2 * g.group() + 2)
                        dve.wait_ge(k_lo_done, 2 * g.group() + 2)
                    dve.tensor_copy(k_next[:, cols], ps).then_inc(piece_freed, 1)
                if kind == G_:
                    dve.wait_ge(piece_half, g.taken(t) + 1)
                    reached(dve, mixed_out[t], 16 * g.stores())
                    dve.tensor_copy(gate[:, cols], ps).then_inc(piece_freed, 1)
                    dve.tensor_scalar(gate_exp[:, cols], gate_exp[:, cols], 1.0, None, ALU.add).then_inc(gate_plus, 1)
                if kind == Q_:
                    dve.wait_ge(piece_half, g.taken(t) + 1)
                    col = qscale[:, bass.ds(g.g + 1, 1)]
                    for m in range(2):
                        own, other = slice(m * HD, (m + 1) * HD), slice((1 - m) * HD, (2 - m) * HD)
                        dve.scalar_tensor_tensor(q_two[other, m, cols], ps[own], col[own], f32(q_two[own, m, cols]),
                                                 ALU.mult, ALU.subtract).then_inc(q_ready, 1)
                    dve.wait_ge(q_ready, 2 * (g.l * 2 * GROUPS + 2 * (g.g + 1) + t % 2 + 1))
                    dve.nop().then_inc(piece_freed, 1)

            def k_lo_part(n, m):
                own = slice(m * HD, (m + 1) * HD)
                dve.wait_ge(k_hi_done, 2 * n + m + 1)
                dve.tensor_tensor(k_lo[own], k_next[own], f32(k_two[own, m]), ALU.subtract).then_inc(k_lo_done, 1)

            def silu(g, t):
                tile = TILE[g.na][t]
                cols = slice(tile * P, (tile + 1) * P)
                if t in (0, STEP0[g.na]):
                    dve.wait_ge(gate_plus, 2 * g.group() + tile // 4 + 1)
                    dve.wait_ge(piece_freed, g.piece(tile // 4) + 1)
                dve.reciprocal(gate_exp[:, cols], gate_exp[:, cols]).then_inc(gate_rec, 1)
                if g.na:
                    dve.wait_ge(gate_rec, g.step(t) + 1)
                    dve.tensor_tensor(gate[:, cols], gate[:, cols], gate_exp[:, cols], ALU.mult)\
                        .then_inc(gate_silu, 1)

            def shifted(g, t, m):
                b, n = t % 2, 2 * g.step(t) + m
                if m == 0:
                    dve.wait_ge(qk_done, g.step(t) + 1)
                    if g.na and t == 0:
                        dve.wait_ge(edge_masked, g.l * NA_G + g.i + 1)
                    begin(dve, "dve")
                w = WIDTH[t] if g.na else S
                if not g.na:
                    bias = dist[:, OFF - t * P:OFF - t * P + S]
                elif INNER[t]:
                    bias = inner[:, m, :]
                else:
                    first = (KEY0[t] - 2 * TILE[True][t] + 6) * W
                    bias = edge[:, m, first:first + w]
                at = window(t, m) if g.na else m * S
                dve.tensor_tensor_reduce(prob[:, b, m, 0:w], all_scores[:, at:at + w], bias, 1.0, -3e38, ALU.add, ALU.max,
                                         mx[:, b, m:m + 1]).then_inc(scores_read, 1)
                reached(dve, scores_read, n + 1)
                scale = -1.0 if g.na else nescale[:, bass.ds(g.i, 1)]
                dve.tensor_scalar(nm[:, b, m:m + 1], mx[:, b, m:m + 1], scale, None, ALU.mult).then_inc(shift_ready, 1)

            def turn_part(g, key, dst, src, hi):
                dve.wait_ge(turn_hi, g.split(*key) + 1)
                dve.tensor_tensor(dst, src, f32(hi), ALU.subtract).then_inc(turn_freed, 1)

            def v_part(g, c):
                tiles, src = v_hl[:, 4 * c:4 * c + 4], turn_bank(g.na, ("V", c))
                if g.na:
                    view = tiles.rearrange("p k (h s e) -> p k h s e", h=2, s=2)
                    hi, lo = view[:, :, :, 0, :], view[:, :, :, 1, :]
                    src = src.rearrange("p (k h e) -> p k h e", k=4, h=2)
                else:
                    hi, lo, src = tiles[:, :, 0:P], tiles[:, :, P:2 * P], src.rearrange("p (k e) -> p k e", k=4)
                turn_part(g, ("V", c), lo, src, hi)

            def p_part(g, t, c):
                src = turn_bank(g.na, ("T", t, c))
                if c == 2:
                    turn_part(g, ("T", t, c), px_lo[:], src[0:HD, 0:256], px_hi[:])
                else:
                    turn_part(g, ("T", t, c), pt_lo[:, c, :], src, pt_hi[:, c, :])

            def combine(g, t):
                b, n = t % 2, g.step(t)
                reached(dve, exp_done, 2 * n + 2)
                dve.reciprocal(rrec[:, b, :], rsum[:, b, :]).then_inc(rrec_done, 1)
                if not g.na:
                    k = g.kind_step(t)
                    dve.wait_ge(rrec_done, n + 1)
                    dve.scalar_tensor_tensor(cmix[:, b:b + 1], rrec[:, b, 1:2], neglam[:, bass.ds(g.l, 1)],
                                             rsum[:, b, 0:1], ALU.mult, ALU.mult).then_inc(cmix_done, 1)
                    dve.wait_ge(cmix_done, k + 1)
                    dve.scalar_tensor_tensor(prob[:, b, 0, :], prob[:, b, 1, :], cmix[:, b:b + 1], prob[:, b, 0, :],
                                             ALU.mult, ALU.add).then_inc(comb_done, 1)

            def output(g, t):
                b, n = t % 2, g.step(t)
                dve.wait_ge(u_half, n + 1)
                if g.na:
                    for m in range(2):
                        cols = slice(m * HD, (m + 1) * HD)
                        last = dve.scalar_tensor_tensor(u[:, b, cols], mix[:, m * P + HD:(m + 1) * P],
                                                        rrec[:, b, m:m + 1], u_hi[:, cols], ALU.mult, ALU.add)
                    last.then_inc(u_done, 1)
                else:
                    dve.scalar_tensor_tensor(u[:, b, :], mix[:, P:2 * P], rrec[:, b, 0:1], u_hi[:], ALU.mult, ALU.add)\
                        .then_inc(u_done, 1)

            def gated(g, t):
                tile, src = TILE[g.na][t], turn_bank(g.na, ("U", t))[:, 0:P]
                cols = slice(tile * P, (tile + 1) * P)
                dve.wait_ge(turned, g.use("U", t) + 1)
                dve.wait_ge(gate_silu, g.step(t) + 1)
                if g.na:
                    dve.tensor_tensor(gate[:, cols], src, gate[:, cols], ALU.mult).then_inc(turn_freed, 1)
                else:
                    dve.scalar_tensor_tensor(gate[:, cols], src, sgain[:, bass.ds(g.l, 1)], gate[:, cols],
                                             ALU.mult, ALU.mult).then_inc(turn_freed, 1)

            def inner_bias(g):
                n = g.l * NA_G + g.i
                dve.wait_ge(edge_masked, n + 1)
                dve.tensor_copy(inner[:], edge[:, :, 2 * W:11 * W]).then_inc(inner_copied, 1)
                dve.wait_ge(inner_copied, n + 1)
                dve.memset(inner[0:W, :, 8 * W:9 * W], MASKED).then_inc(inner_ready, 1)
                dve.memset(inner[W:P, :, 0:W], MASKED).then_inc(inner_ready, 1)
                dve.wait_ge(inner_ready, 2 * n + 2)

            def take_mixed(l, i):
                dve.wait_ge(h_hi_done, l * (2 * NT + 1) + NT + i + 1)
                dve.tensor_tensor(h_lo[:, i, :], f32(h_lo[:, i, :]), f32(h_hi[:, i, :]), ALU.subtract)\
                    .then_inc(h_ready, 1)

            def attend(g, behind):
                for t, front, ft in steps(g, behind):
                    if front:
                        for m in range(2):
                            shifted(front, ft, m)
                    def add_pieces(slot):
                        if not behind and slot < len(LAST_FILL[t]):
                            for p, ks in LAST_FILL[t][slot]:
                                if NT - 2 in ks:
                                    add_piece(g.l, p, p)

                    for c in range(3 if g.na and INNER[t - 1] else 2):
                        if c < 2:
                            add_pieces(c)
                        p_part(g, t - 1, c)
                        if g.project and t == NT - 1 and c < 2:
                            k_lo_part(g.group() + 1, c)
                    if front:
                        combine(front, ft)
                    if front and front.projects(ft) and ft:
                        piece_part(front, ft)
                    silu(g, t - 1)
                    add_pieces(2)
                    if t >= 2:
                        gated(g, t - 2)
                    output(g, t - 1)
                    add_pieces(3)
                    if g.na and t == 2:
                        inner_bias(g)
                    if t == NT and behind:
                        for c in range(2):
                            v_part(behind, c)
                        piece_part(behind, 0)
                    if not behind:
                        for i in TAKEN.get(t, ()):
                            take_mixed(g.l, i)
                gated(g, NT - 1)

            def add_piece(l, i, t):
                reached(dve, piece_done, l * PPL + IN + i + 1)
                dve.tensor_tensor(xt[:, t // 2, half(t)], xt[:, t // 2, half(t)], proj[:, i % 2], ALU.add)\
                    .then_inc(piece_freed, 1)

            with dve.Fori(0, DEPTH) as l:
                norm_stats(l)
                first = First(l)

                def lo_of(i):
                    dve.wait_ge(h_hi_done, l * (2 * NT + 1) + i + 1)
                    dve.tensor_tensor(h_lo[:, i, :], normed[i % 4], f32(h_hi[:, i, :]), ALU.subtract)\
                        .then_inc(h_ready, 1)

                for i in range(NT):
                    if i >= 4:
                        norm_ready(dve, l, i - 4)
                    dve.scalar_tensor_tensor(normed[i % 4], xt[:, i, :], ngain[:, bass.ds(l * NT + i, 1)],
                                             scores[:, 0, :], ALU.mult, ALU.mult).then_inc(norm_done, 1)
                    if i % 2:
                        lo_of(i - 1)
                for t in First.STEPS:
                    piece_part(first, t)
                    if t == 2 * K_ + 1:
                        for m in range(2):
                            k_lo_part(l * GROUPS, m)
                g = Group(l, False, 0)
                for c in range(2):
                    shifted(g, 0, c)
                for c in range(2):
                    v_part(g, c)
                combine(g, 0)
                piece_part(g, 0)
                reached(dve, turn_freed, g.use("V", 1) + 1)
                dve.sem_inc(turn_freed, 1)
                groups(dve, l, attend)
                for hf in range(2):
                    dve.wait_ge(h_hi_done, l * (2 * NT + 1) + 2 * NT + hf)
                    dve.tensor_tensor(h_lo[:, NT - 1, half(hf)], gate[:, half(hf)], f32(h_hi[:, NT - 1, half(hf)]),
                                      ALU.subtract).then_inc(h_ready, 1)
                for q, t in enumerate(LATE):
                    add_piece(l, EARLY + q, t)
            norm_stats(DEPTH)
            for i in range(NT):
                if i >= 4:
                    dve.wait_ge(stored[i % 4], 16)
                dve.scalar_tensor_tensor(normed[i % 4], xt[:, i, :], fgain[:, i:i + 1], scores[:, 0, :],
                                         ALU.mult, ALU.mult).then_inc(norm_done, 1)


def kernel(x, norm_g, w_in, w_out, lam_q1, lam_k1, lam_q2, lam_k2, subln_g, rpb, final_g):
    import concourse.bacc as bacc
    from concourse.bass_utils import run_bass_kernel_spmd

    f = lambda a: np.asarray(a)
    x, norm_g, w_in, w_out, subln_g, rpb, final_g = map(f, (x, norm_g, w_in, w_out, subln_g, rpb, final_g))
    depth, D, _ = w_in.shape
    S = x.shape[1]
    cut = lambda w: w.reshape(depth, D // P, P, -1, P).transpose(0, 3, 2, 1, 4)
    by_out = cut(w_in)
    q, k, v = [list(range(4 * j, 4 * j + 4)) + list(range(12 + 4 * j, 16 + 4 * j)) for j in range(3)]
    order = [v[0], k[0], q[0]]
    for g in range(8):
        order += [24 + g] + ([v[g + 1], k[g + 1], q[g + 1]] if g < 7 else [])
    out_chunks, last_rows = cut(w_out), w_out[:, -P:].reshape(depth, 1, P, D // P, P)
    stream = np.concatenate([by_out[:, order], out_chunks[:, :5], last_rows, out_chunks[:, 5:]],
                            axis=1).reshape(-1, P, D)
    stream = np.concatenate([stream, stream[:2]])
    gap = np.zeros(64, rpb.dtype)
    columns = lambda a: np.ascontiguousarray(a.reshape(-1, P).T)
    arrays = {
        "x_t": x[0].T,
        "chunks": stream,
        "norm_gain": columns(norm_g),
        "final_gain": columns(final_g),
        "subln_gain": columns(subln_g),
        "lam_vecs": np.stack([f(lam_q1), f(lam_k1), f(lam_q2), f(lam_k2)])[None],
        "bias_rows": np.concatenate([gap, rpb.ravel(), gap]),
    }
    arrays = {n: np.ascontiguousarray(a) for n, a in arrays.items()}
    nc = bacc.Bacc("TRN2", target_bir_lowering=False, num_devices=1)
    aps = [nc.dram_tensor(n, a.shape, mybir.dt.from_np(a.dtype), kind="ExternalInput").ap() for n, a in arrays.items()]
    out = nc.dram_tensor("out_t", (D, S), F32, kind="ExternalOutput").ap()
    hybrid_encoder(nc, *aps, out)
    r = run_bass_kernel_spmd(nc, [arrays], core_ids=[0])
    return np.ascontiguousarray(r.results[0]["out_t"].T)[None]
```
